# Optimizing a Trainium2 kernel written in Bass

```python
import jax, jax.numpy as jnp
from jax import lax
import numpy as np

D_MODEL = 1024
BATCH = 1
SEQ = 256
DEPTH = 1
DEC_BATCH = 1
DEC_SEQ = 1024
PAST_LEN = 128

N_ATTN_HEADS = 8
N_KV_HEADS = 2
ATTN_HEAD_DIM = 64
WINDOW = 128
ATTN_BLOCK = 128
ROPE_THETA = 10000.0
N_GLA_HEADS = 4
GLA_KEY_DIM = 64
GLA_VALUE_DIM = 128
GLA_GATE_RANK = 16
GLA_GATE_NORMALIZER = 16.0
GLA_CHUNK = 64
D_FF = 2816
EPS = 1e-6

ATTN_Q = N_ATTN_HEADS * ATTN_HEAD_DIM
ATTN_KV = N_KV_HEADS * ATTN_HEAD_DIM
GLA_QK = N_GLA_HEADS * GLA_KEY_DIM
GLA_V = N_GLA_HEADS * GLA_VALUE_DIM
MIX_WIDTH = ATTN_Q + GLA_V
IN_SPLIT_OFFSETS = [ATTN_Q, ATTN_Q + ATTN_KV, ATTN_Q + 2 * ATTN_KV, ATTN_Q + 2 * ATTN_KV + GLA_QK, ATTN_Q + 2 * ATTN_KV + 2 * GLA_QK, ATTN_Q + 2 * ATTN_KV + 2 * GLA_QK + GLA_V, ATTN_Q + 2 * ATTN_KV + 2 * GLA_QK + 2 * GLA_V, ATTN_Q + 2 * ATTN_KV + 2 * GLA_QK + 2 * GLA_V + GLA_GATE_RANK]
IN_PROJ_WIDTH = ATTN_Q + 2 * ATTN_KV + 2 * GLA_QK + 2 * GLA_V + 2 * GLA_GATE_RANK

kernel_name = 'hymba_swa_gla_macaron_encoder'

def rmsnorm(x, gain):
    xf = x.astype(jnp.float32)
    y = xf * lax.rsqrt(jnp.mean(xf * xf, axis=-1, keepdims=True) + EPS)
    return (y * gain.astype(jnp.float32)).astype(x.dtype)

def swiglu(h, w_gate, w_up, w_down):
    return (jax.nn.silu(h @ w_gate) * (h @ w_up)) @ w_down

def rotary(x):
    T, d = x.shape[1], x.shape[-1]
    half = d // 2
    inv_freq = ROPE_THETA ** (-jnp.arange(half, dtype=jnp.float32) / half)
    ang = jnp.arange(T, dtype=jnp.float32)[:, None] * inv_freq[None, :]
    cos = jnp.cos(ang)[None, :, None, :]
    sin = jnp.sin(ang)[None, :, None, :]
    xf = x.astype(jnp.float32)
    x1, x2 = xf[..., :half], xf[..., half:]
    return jnp.concatenate([x1 * cos - x2 * sin, x2 * cos + x1 * sin], axis=-1).astype(x.dtype)

def windowed_gqa_attention(q, k, v, sink):
    B, T, Hq, d = q.shape
    nb = T // ATTN_BLOCK
    G = Hq // N_KV_HEADS
    pad = ((0, 0), (ATTN_BLOCK, ATTN_BLOCK), (0, 0), (0, 0))
    kp = jnp.pad(k, pad).reshape(B, nb + 2, ATTN_BLOCK, N_KV_HEADS, d)
    vp = jnp.pad(v, pad).reshape(B, nb + 2, ATTN_BLOCK, N_KV_HEADS, d)
    kw = jnp.concatenate([kp[:, :-2], kp[:, 1:-1], kp[:, 2:]], axis=2)
    vw = jnp.concatenate([vp[:, :-2], vp[:, 1:-1], vp[:, 2:]], axis=2)
    qb = q.reshape(B, nb, ATTN_BLOCK, N_KV_HEADS, G, d)
    s = jnp.einsum('bnqhgd,bnkhd->bnhgqk', qb, kw).astype(jnp.float32) * (d ** -0.5)
    i = jnp.arange(ATTN_BLOCK)[:, None]
    j = jnp.arange(3 * ATTN_BLOCK)[None, :]
    rel = j - ATTN_BLOCK - i
    kpos = (jnp.arange(nb)[:, None, None] - 1) * ATTN_BLOCK + j[None]
    mask = (jnp.abs(rel)[None] <= WINDOW) & (kpos >= 0) & (kpos < T)
    mask = mask[None, :, None, None, :, :]
    s = jnp.where(mask, s, -1e30)
    sink_b = sink.astype(jnp.float32).reshape(N_KV_HEADS, G)[None, None, :, :, None, None]
    m = jnp.maximum(jnp.max(s, axis=-1, keepdims=True), sink_b)
    p = jnp.where(mask, jnp.exp(s - m), 0.0)
    denom = jnp.sum(p, axis=-1, keepdims=True) + jnp.exp(sink_b - m)
    probs = (p / denom).astype(v.dtype)
    o = jnp.einsum('bnhgqk,bnkhd->bnqhgd', probs, vw)
    return o.reshape(B, T, Hq * d)

def gla_chunked(q, k, v, log_a, strict):
    B, H, T, dk = q.shape
    dv = v.shape[-1]
    C = GLA_CHUNK
    n = T // C
    q = q.reshape(B, H, n, C, dk)
    k = k.reshape(B, H, n, C, dk)
    v = v.reshape(B, H, n, C, dv)
    b = jnp.cumsum(log_a.reshape(B, H, n, C, dk), axis=3)
    b_last = b[:, :, :, -1:, :]
    q_e = q * jnp.exp(b)
    k_e = k * jnp.exp(-b)
    tri = jnp.tril(jnp.ones((C, C), jnp.float32), k=-1 if strict else 0)
    A = jnp.einsum('bhnid,bhnjd->bhnij', q_e, k_e) * tri
    o_intra = jnp.einsum('bhnij,bhnjv->bhniv', A, v)
    k_s = k * jnp.exp(b_last - b)
    U = jnp.einsum('bhnjd,bhnjv->bhndv', k_s, v)
    decay = jnp.exp(b_last[:, :, :, 0, :])

    def step(S, inp):
        dec, u = inp
        return dec[..., None] * S + u, S

    S0 = jnp.zeros((B, H, dk, dv), jnp.float32)
    _, S_prev = lax.scan(step, S0, (jnp.moveaxis(decay, 2, 0), jnp.moveaxis(U, 2, 0)))
    S_prev = jnp.moveaxis(S_prev, 0, 2)
    o_inter = jnp.einsum('bhnid,bhndv->bhniv', q_e, S_prev)
    return (o_intra + o_inter).reshape(B, H, T, dv)

def hybrid_mixer(h, w_in, attn_sink, w_gla_decay_fwd, b_gla_decay_fwd, w_gla_decay_bwd, b_gla_decay_bwd, gla_out_norm, w_out):
    B, T, _ = h.shape
    proj = h @ w_in
    aq, ak, av, gq, gk, gv, gg, r_f, r_b = jnp.split(proj, IN_SPLIT_OFFSETS, axis=-1)
    aq = rotary(aq.reshape(B, T, N_ATTN_HEADS, ATTN_HEAD_DIM))
    ak = rotary(ak.reshape(B, T, N_KV_HEADS, ATTN_HEAD_DIM))
    av = av.reshape(B, T, N_KV_HEADS, ATTN_HEAD_DIM)
    o_attn = windowed_gqa_attention(aq, ak, av, attn_sink)

    def to_heads(t, dh):
        return t.reshape(B, T, -1, dh).transpose(0, 2, 1, 3).astype(jnp.float32)

    q_g = to_heads(gq, GLA_KEY_DIM) * (GLA_KEY_DIM ** -0.5)
    k_g = to_heads(gk, GLA_KEY_DIM)
    v_g = to_heads(gv, GLA_VALUE_DIM)
    la_f = to_heads(jax.nn.log_sigmoid((r_f @ w_gla_decay_fwd + b_gla_decay_fwd).astype(jnp.float32)) / GLA_GATE_NORMALIZER, GLA_KEY_DIM)
    la_b = to_heads(jax.nn.log_sigmoid((r_b @ w_gla_decay_bwd + b_gla_decay_bwd).astype(jnp.float32)) / GLA_GATE_NORMALIZER, GLA_KEY_DIM)
    o_f = gla_chunked(q_g, k_g, v_g, la_f, False)
    o_b = jnp.flip(gla_chunked(jnp.flip(q_g, 2), jnp.flip(k_g, 2), jnp.flip(v_g, 2), jnp.flip(la_b, 2), True), 2)
    o_g = (o_f + o_b).transpose(0, 2, 1, 3)
    o_g = rmsnorm(o_g, gla_out_norm) * jax.nn.silu(gg.astype(jnp.float32).reshape(B, T, N_GLA_HEADS, GLA_VALUE_DIM))
    o_gla = o_g.reshape(B, T, GLA_V).astype(h.dtype)

    return jnp.concatenate([o_attn, o_gla], axis=-1) @ w_out

def encoder_trunk(x, norm_ffn1, w_ffn1_gate, w_ffn1_up, w_ffn1_down, norm_mix, w_in, attn_sink, w_gla_decay_fwd, b_gla_decay_fwd, w_gla_decay_bwd, b_gla_decay_bwd, gla_out_norm, w_out, norm_ffn2, w_ffn2_gate, w_ffn2_up, w_ffn2_down, norm_final):
    for l in range(DEPTH):
        x = x + 0.5 * swiglu(rmsnorm(x, norm_ffn1[l]), w_ffn1_gate[l], w_ffn1_up[l], w_ffn1_down[l])
        x = x + hybrid_mixer(rmsnorm(x, norm_mix[l]), w_in[l], attn_sink[l], w_gla_decay_fwd[l], b_gla_decay_fwd[l], w_gla_decay_bwd[l], b_gla_decay_bwd[l], gla_out_norm[l], w_out[l])
        x = x + 0.5 * swiglu(rmsnorm(x, norm_ffn2[l]), w_ffn2_gate[l], w_ffn2_up[l], w_ffn2_down[l])
    return rmsnorm(x, norm_final)

def setup_inputs(seed: int = 0) -> dict:
    key = jax.random.key(seed)
    ks = jax.random.split(key, 24)
    f32 = jnp.float32

    def w(k, shape, fan_in):
        return jax.random.normal(k, shape, f32) * (fan_in ** -0.5)

    def gain(k, shape):
        return 1.0 + 0.01 * jax.random.normal(k, shape, f32)

    return {
        'x_prompt': jax.random.normal(ks[0], (BATCH, SEQ, D_MODEL), f32),
        'x_sample': jax.random.normal(ks[1], (DEC_BATCH, DEC_SEQ, D_MODEL), f32),
        'norm_ffn1': gain(ks[2], (DEPTH, D_MODEL)),
        'w_ffn1_gate': w(ks[3], (DEPTH, D_MODEL, D_FF), D_MODEL),
        'w_ffn1_up': w(ks[4], (DEPTH, D_MODEL, D_FF), D_MODEL),
        'w_ffn1_down': w(ks[5], (DEPTH, D_FF, D_MODEL), D_FF),
        'norm_mix': gain(ks[6], (DEPTH, D_MODEL)),
        'w_in': w(ks[7], (DEPTH, D_MODEL, IN_PROJ_WIDTH), D_MODEL),
        'attn_sink': 0.5 * jax.random.normal(ks[8], (DEPTH, N_ATTN_HEADS), f32),
        'w_gla_decay_fwd': w(ks[9], (DEPTH, GLA_GATE_RANK, GLA_QK), GLA_GATE_RANK),
        'b_gla_decay_fwd': 0.1 * jax.random.normal(ks[10], (DEPTH, GLA_QK), f32),
        'w_gla_decay_bwd': w(ks[11], (DEPTH, GLA_GATE_RANK, GLA_QK), GLA_GATE_RANK),
        'b_gla_decay_bwd': 0.1 * jax.random.normal(ks[12], (DEPTH, GLA_QK), f32),
        'gla_out_norm': gain(ks[13], (DEPTH, GLA_VALUE_DIM)),
        'w_out': w(ks[14], (DEPTH, MIX_WIDTH, D_MODEL), MIX_WIDTH),
        'norm_ffn2': gain(ks[15], (DEPTH, D_MODEL)),
        'w_ffn2_gate': w(ks[16], (DEPTH, D_MODEL, D_FF), D_MODEL),
        'w_ffn2_up': w(ks[17], (DEPTH, D_MODEL, D_FF), D_MODEL),
        'w_ffn2_down': w(ks[18], (DEPTH, D_FF, D_MODEL), D_FF),
        'norm_final': gain(ks[19], (D_MODEL,)),
    }

def reference(x_prompt, x_sample, norm_ffn1, w_ffn1_gate, w_ffn1_up, w_ffn1_down, norm_mix, w_in, attn_sink, w_gla_decay_fwd, b_gla_decay_fwd, w_gla_decay_bwd, b_gla_decay_bwd, gla_out_norm, w_out, norm_ffn2, w_ffn2_gate, w_ffn2_up, w_ffn2_down, norm_final):
    y_prompt = encoder_trunk(x_prompt, norm_ffn1, w_ffn1_gate, w_ffn1_up, w_ffn1_down, norm_mix, w_in, attn_sink, w_gla_decay_fwd, b_gla_decay_fwd, w_gla_decay_bwd, b_gla_decay_bwd, gla_out_norm, w_out, norm_ffn2, w_ffn2_gate, w_ffn2_up, w_ffn2_down, norm_final)
    y_sample = encoder_trunk(x_sample, norm_ffn1, w_ffn1_gate, w_ffn1_up, w_ffn1_down, norm_mix, w_in, attn_sink, w_gla_decay_fwd, b_gla_decay_fwd, w_gla_decay_bwd, b_gla_decay_bwd, gla_out_norm, w_out, norm_ffn2, w_ffn2_gate, w_ffn2_up, w_ffn2_down, norm_final)
    return (y_prompt, y_sample)


_drawn_inputs = setup_inputs


def setup_inputs(seed=0):
    import zlib

    import numpy as np

    out = dict(_drawn_inputs(seed))
    spreads = {}
    factors = {'norm_ffn1': 8.0,
     'norm_mix': 6.739,
     'attn_sink': 8.0,
     'b_gla_decay_fwd': 4.622,
     'b_gla_decay_bwd': 4.784,
     'gla_out_norm': 8.0,
     'norm_ffn2': 8.0,
     'norm_final': 5.676}
    for name, (base, spread) in spreads.items():
        noise = np.random.default_rng([zlib.crc32(name.encode()), seed]).standard_normal(out[name].shape)
        drawn = base * np.exp(spread * noise) if base else spread * noise
        out[name] = __import__('jax').numpy.asarray(drawn.astype(out[name].dtype))
    for name, factor in factors.items():
        out[name] = (out[name] * factor).astype(out[name].dtype)
    return out
```

```python
from contextlib import ExitStack

import concourse.bass as bass
import numpy as np
from concourse import mybir

F32 = mybir.dt.float32
F32R = mybir.dt.float32r
BF16 = mybir.dt.bfloat16
ALU = mybir.AluOpType
ACT = mybir.ActivationFunctionType
AX = mybir.AxisListType

P = 128
D_MODEL = 1024
KT = D_MODEL // P
SEQS = (256, 1024)
TOK = sum(SEQS)
TT = TOK // P
D_FF = 2816
GROUPS = D_FF // (2 * P)
CHUNKS = ((0, 512), (512, 512), (1024, 256))
NCH = len(CHUNKS)
NORM_COLS = 256
NORM_STEPS = TOK // NORM_COLS
EPS = 1e-6

HEADS, KV, HD = 8, 2, 64
HPG = HEADS // KV
GLA_HEADS, DK, DV, RANK = 4, 64, 128, 16
GATE_NORM = 16.0
C = 64
SEQ_CHUNKS = tuple(s // C for s in SEQS)
ROW_AK = HEADS * HD
ROW_AV = ROW_AK + KV * HD
ROW_GQ = ROW_AV + KV * HD
ROW_GK = ROW_GQ + GLA_HEADS * DK
ROW_GV = ROW_GK + GLA_HEADS * DK
ROW_GG = ROW_GV + GLA_HEADS * DV
ROW_R = ROW_GG + GLA_HEADS * DV
IN_W = ROW_R + 2 * RANK
IN_TILES = IN_W // P

ROW_E = IN_TILES * P

RAW, SPLIT = 3, 3
U_IN = 6 * GROUPS
U_OUT = U_IN + 1 + IN_TILES
U_FFN2 = U_OUT + KT
U_END = U_FFN2 + 6 * GROUPS
NEG = -1e30


def build(nc, x_prompt, x_sample, norm_ffn1, w_ffn1_gate, w_ffn1_up, w_ffn1_down, norm_mix, w_in, attn_sink,
          w_gla_decay_fwd, b_gla_decay_fwd, w_gla_decay_bwd, b_gla_decay_bwd, gla_out_norm, w_out, norm_ffn2,
          w_ffn2_gate, w_ffn2_up, w_ffn2_down, norm_final, c_ident, c_cos, c_sin, c_window, c_gla_masks, c_reset,
          y_prompt, y_sample, proj):
    ctx = ExitStack()
    with ctx:
        def sb(name, shape, dt=F32, scope=ctx):
            return scope.enter_context(nc.sbuf_tensor(name, shape, dt))

        def sem(name):
            return ctx.enter_context(nc.semaphore(name))

        xT = sb("xT", [P, KT, TOK])
        w_raw = [sb(f"w_raw{s}", [P, KT, P]) for s in range(RAW)]
        w_hi = [sb(f"w_hi{s}", [P, KT, P], F32R) for s in range(SPLIT)]
        w_lo = [sb(f"w_lo{s}", [P, KT, P], F32R) for s in range(SPLIT)]
        ident = sb("ident", [P, P])
        ident_bf = sb("ident_bf", [P, P], BF16)
        ones = sb("ones", [P, P])
        gains = sb("gains", [P, 4, KT])
        gla_gain = sb("gla_gain", [P, 1])
        sinks = sb("sinks", [P, HEADS])
        neg_sinks = sb("neg_sinks", [P, HEADS])

        with ExitStack() as s:
            hid_hi = sb("hid_hi", [P, 2, TOK], F32R, s)
            hid_lo = sb("hid_lo", [P, 2, TOK], F32R, s)
            scaled_g, scaled_u, silu, prod = ([sb(f"{n}{j}", [P, 512], scope=s) for j in range(2)]
                                              for n in ("scaled_g", "scaled_u", "silu", "prod"))
        with ExitStack() as s:
            stage = [sb(f"stage{j}", [P, TOK], scope=s) for j in range(3)]
        with ExitStack() as s:
            s.enter_context(nc.sbuf_tensor("under_stage", [P, 3, TOK], F32))
            rT = sb("rT", [2 * RANK + 1, TOK], scope=s)
            reset = sb("reset", [P, TOK], scope=s)
            gla_z = sb("gla_z", [P, TOK], scope=s)
            gla_t = sb("gla_t", [P, TOK], scope=s)
            gla_b = sb("gla_b", [P, TOK], scope=s)
        with ExitStack() as s:
            gla_s = [sb(f"gla_s{j}", [P, DV, TOK // C], scope=s) for j in range(2)]
        with ExitStack() as s:
            x_in = [sb(f"x_in{j}", [P, D_MODEL], scope=s) for j in range(4)]
        with ExitStack() as s:
            y_out = [sb(f"y_out{j}", [P, D_MODEL], scope=s) for j in range(2)]
            normed = [sb(f"normed{j}", [P, KT, P], scope=s) for j in range(2)]
        o_raw = sb("o_raw", [P, KT, TOK])
        with ExitStack() as s:
            h_hi = sb("h_hi", [P, KT, TOK], F32R, s)
            h_lo = sb("h_lo", [P, KT, TOK], F32R, s)
            rstd = sb("rstd", [P, TOK], scope=s)
            with ExitStack() as r:
                square = [sb(f"square{j}", [P, CHUNKS[j][1]], scope=r) for j in range(NCH)]
            w_dec = sb("w_dec", [2 * RANK + 1, P], scope=s)
        with ExitStack() as s:
            gq = [sb(f"gq{j}", [P, TOK], scope=s) for j in range(2)]
            e_fw = [sb(f"e_fw{j}", [P, TOK], scope=s) for j in range(2)]
            k_in = [sb(f"k_in{j}", [P, TOK], scope=s) for j in range(2)]
            k_out = [sb(f"k_out{j}", [P, TOK], scope=s) for j in range(2)]
            gk = sb("gk", [P, TOK], scope=s)
            gvT = sb("gvT", [P, TOK], scope=s)
            gla_vn = [sb(f"gla_vn{j}", [P, TT, DV], scope=s) for j in range(2)]
            gla_kn = sb("gla_kn", [P, TT, P], scope=s)
            gla_a = [sb(f"gla_a{j}", [P, TT, P], scope=s) for j in range(2)]
            gla_dec = sb("gla_dec", [P, DV, TOK // C], scope=s)
            masks = sb("masks", [P, 2, P], scope=s)
        with ExitStack() as s:
            gg = sb("gg", [P, GLA_HEADS, TOK], scope=s)
            gsq = [sb(f"gsq{j}", [P, 512], scope=s) for j in range(3)]
            grs = [sb(f"grs{j}", [P, 512], scope=s) for j in range(3)]
        with ExitStack() as s:
            q_in = [sb(f"q_in{j}", [HD, HEADS, P], scope=s) for j in range(2)]
            q_sw = [sb(f"q_sw{j}", [HD, HEADS, P], scope=s) for j in range(2)]
            q_rot = [sb(f"q_rot{j}", [HD, HEADS, P], scope=s) for j in range(2)]
            kT = sb("kT", [HD, KV, TOK + 2 * P], scope=s)
            vN = sb("vN", [P, TT + 2, P], scope=s)
            window = sb("window", [P, TT, 2, P], BF16, s)
            cos = sb("cos", [HD, TOK], scope=s)
            sin = sb("sin", [HD, TOK], scope=s)
            probsT = sb("probsT", [P, 2, 3, P], scope=s)
            o_nat = [sb(f"o_nat{j}", [P, P], scope=s) for j in range(2)]
            stats = [sb(f"stats{j}", [P, 6, 2], scope=s) for j in range(4)]
            with ExitStack() as r:
                probs = [sb(f"probs{j}", [P, 2, 3 * P], scope=r) for j in range(4)]
            with ExitStack() as r:
                vT = sb("vT", [P, TOK], scope=r)
                k_sw = sb("k_sw", [HD, KV, TOK], scope=r)
                window_f = sb("window_f", [P, TT, 2, P], scope=r)
        MX, NEGM, DSINK, SUM, ESINK, RDEN = range(6)

        ps = ctx.enter_context(nc.psum_tensor("ps", [P, 8, 512], F32))
        GU, DN = 0, 4
        O_BANKS = (2, 3, 7)
        SUMS = (2, 3, 2)
        psf = ps[:, :, :].rearrange("p b n -> p (b n)")

        ld_const, const_bf, const_ones, const_neg = (sem(n) for n in ("ld_const", "const_bf", "const_ones", "const_neg"))
        w_loaded = [sem(f"w_loaded{s}") for s in range(RAW)]
        w_hi_ready, w_lo_ready = sem("w_hi_ready"), sem("w_lo_ready")
        LO = RAW
        x_loaded = [sem(f"x_loaded{j}") for j in range(4)]
        x_turned, x_kept_act, x_kept_dve = sem("x_turned"), sem("x_kept_act"), sem("x_kept_dve")

        def named(prefix, names):
            return {k: sem(f"{prefix}_{k}") for k in names.split()}

        norm_names = "square sum mean sqrt rstd hi lo"
        N1, NM, N2, NF = (named(n, norm_names) for n in ("norm_ffn1", "norm_mix", "norm_ffn2", "norm_final"))
        ffn_names = "gate_used gu_done gate_rs up_rs silu prod hid_hi hid_lo dn_done dn_added"
        A1, A2 = named("ffn1", ffn_names), named("ffn2", ffn_names)
        GU_FREE, DN_USED, DN_FREE = 2, 1, 4
        in_done, in_moved = sem("in_done"), sem("in_moved")
        IN_USED, IN_FREE = 2 * NCH, NCH
        GATE_FREE = NCH
        in_stored = [sem(f"in_stored{j}") for j in range(3)]
        o_hi, o_lo, out_done, out_added = (sem(n) for n in ("o_hi", "o_lo", "out_done", "out_added"))
        G = named("gla", "zeroed ones w_ld ld_reset ld_masks gate z abs exp ln log scan eb enb diff es e_stored ld_k ld_v "
                         "qe ks ke decay s_zeroed vT vN kT kN scores masked_f masked_b masked u u_fw u_bw state o o_kept")
        g_ld = [sem(f"gla_ld{j}") for j in range(2)]
        gn = named("gla_norm", "ld silu square sum mean sqrt rstd scaled gated")
        T = named("attn", "ld pads cosd sind keys vT vN window qcos qsin qrot s max negm dsink p es den rden turned "
                          "pT_act pT_dve pv o_nat oT o_kept")
        S_FREE, P_FREE, PT_FREE, ON_FREE, OT_FREE = 8, 4, 1, 2, 1
        t_ld = [sem(f"attn_ld{j}") for j in range(2)]
        y_scaled, y_turned, y_kept = sem("y_scaled"), sem("y_turned"), sem("y_kept")
        y_stored = [sem(f"y_stored{j}") for j in range(2)]
        N_CONST_LD = 7

        def col_unit(w, col, cols=P):
            return w[0].rearrange("(k p) n -> p k n", p=P)[:, :, bass.ds(col, cols)]

        def row_unit(w, row):
            return w[0][bass.ds(row, P), :].rearrange("p (k n) -> p k n", k=KT)

        def u_col(n):
            return (2 + 3 * (n % 2)) * 512 + n // 2 * DV

        first_chunks = (0, SEQ_CHUNKS[0])
        last_chunks = (SEQ_CHUNKS[0] - 1, TOK // C - 1)

        block = ctx.enter_context(nc.Block())

        @block.sync
        def _(sp):
            sp.dma_start(ident[:, :], c_ident).then_inc(ld_const, 16)

            def x_load(t):
                src = x_prompt[0][t * P:(t + 1) * P, :] if t < 2 else x_sample[0][(t - 2) * P:(t - 1) * P, :]
                sp.dma_start(x_in[t % 4][:, :], src).then_inc(x_loaded[t % 4], 16)

            for t in range(4):
                x_load(t)
            with nc.allow_non_contiguous_dma(reason="small parameter columns"):
                for n, g in enumerate((norm_ffn1[0], norm_mix[0], norm_ffn2[0], norm_final)):
                    sp.dma_start(gains[:, n, :], g.rearrange("(k p) -> p k", p=P)).then_inc(ld_const, 16)
                sp.dma_start(gla_gain[:, :], gla_out_norm.rearrange("a p -> p a")).then_inc(ld_const, 16)
            sp.dma_start(sinks[:, :], attn_sink[0:1, :].to_broadcast([P, HEADS])).then_inc(ld_const, 16)

            def load_unit(unit, slot, src, cols=P):
                sp.wait_ge(w_lo_ready, unit + 1)
                sp.dma_start(w_raw[slot][:, :, 0:cols], src).then_inc(w_loaded[slot], 16)

            def ffn_units(base, wg, wu, wd, i):
                for j, src in enumerate((col_unit(wg, i * 2 * P), col_unit(wu, i * 2 * P),
                                         col_unit(wg, i * 2 * P + P), col_unit(wu, i * 2 * P + P),
                                         row_unit(wd, i * 2 * P), row_unit(wd, i * 2 * P + P))):
                    load_unit(base + j + 6 * i, j % RAW, src)

            for j, w in enumerate((w_ffn1_gate, w_ffn1_up)):
                load_unit(j, j, col_unit(w, 0))
            for t in range(4, TT):
                sp.wait_ge(x_turned, 2 * (t - 3))
                x_load(t)
            for j, src in enumerate((col_unit(w_ffn1_gate, P), col_unit(w_ffn1_up, P),
                                     row_unit(w_ffn1_down, 0), row_unit(w_ffn1_down, P)), 2):
                load_unit(j, j % RAW, src)
            with sp.Fori(1, GROUPS) as i:
                ffn_units(0, w_ffn1_gate, w_ffn1_up, w_ffn1_down, i)
            load_unit(U_IN, 0, col_unit(w_in, ROW_R, 2 * RANK), 2 * RANK)
            with sp.Fori(0, IN_TILES // 3) as i:
                for j in range(3):
                    load_unit(U_IN + 1 + 3 * i + j, (1 + j) % RAW, col_unit(w_in, i * 3 * P + j * P))
            for u in range(U_OUT, U_OUT + RAW):
                load_unit(u, u % RAW, col_unit(w_out, (u - U_OUT) * P))

            for j in range(3):
                sp.wait_ge(in_stored[j], 16 + 16 * IN_TILES // 3)
            sp.wait_ge(G["e_stored"], 48 * (GLA_HEADS + 1))
            sp.wait_ge(in_done, IN_USED + NCH * (IN_TILES + 1))

            def gla_loads(h):
                p = h % 2
                for half in range(2):
                    rows = slice(half * DK, (half + 1) * DK)
                    sp.dma_start(gq[p][rows, :], proj[h * DK + ROW_GQ:(h + 1) * DK + ROW_GQ, :]).then_inc(g_ld[p], 16)
                for e, to in enumerate((e_fw, k_in, k_out)):
                    row = ROW_E + (3 * h + e) * P
                    sp.dma_start(to[p][:, :], proj[row:row + P, :]).then_inc(g_ld[p], 16)

            def load_k(h):
                for half in range(2):
                    sp.dma_start(gk[half * DK:(half + 1) * DK, :], proj[h * DK + ROW_GK:(h + 1) * DK + ROW_GK, :]
                                 ).then_inc(G["ld_k"], 16)

            def load_v(h):
                sp.dma_start(gvT[:, :], proj[h * DV + ROW_GV:(h + 1) * DV + ROW_GV, :]).then_inc(G["ld_v"], 16)

            load_v(0)
            load_k(0)
            gla_loads(0)
            sp.dma_start(masks[:, :, :], c_gla_masks.rearrange("m p n -> p m n")).then_inc(G["ld_masks"], 16)
            gla_loads(1)
            for h in range(1, GLA_HEADS):
                sp.wait_ge(G["vT"], NCH * h)
                load_v(h)
                sp.wait_ge(G["ks"], h)
                sp.wait_ge(G["ke"], h)
                load_k(h)
                if h + 1 < GLA_HEADS:
                    sp.wait_ge(G["o"], NCH * h)
                    sp.wait_ge(G["decay"], 4 * h)
                    gla_loads(h + 1)
            sp.wait_ge(G["o"], NCH * GLA_HEADS)
            for h in range(GLA_HEADS):
                sp.dma_start(gg[:, h, :], proj[ROW_GG + h * DV:ROW_GG + (h + 1) * DV, :]).then_inc(gn["ld"], 16)

            sp.wait_ge(gn["gated"], NCH * GLA_HEADS)
            ak = proj[ROW_AK:ROW_AK + KV * HD, :].rearrange("(g d) n -> d g n", d=HD)
            aq = proj[0:HEADS * HD, :].rearrange("(h d) n -> d h n", d=HD)
            halves = [(slice(a * HD // 2, (a + 1) * HD // 2), slice((1 - a) * HD // 2, (2 - a) * HD // 2)) for a in range(2)]
            sp.dma_start(kT[:, :, P:P + TOK], ak).then_inc(T["ld"], 16)
            for to, of in halves:
                sp.dma_start(k_sw[to, :, :], ak[of, :, :]).then_inc(T["ld"], 16)
            sp.dma_start(vT[:, :], proj[ROW_AV:ROW_AV + KV * HD, :]).then_inc(T["ld"], 16)
            sp.dma_start(cos[:, :], c_cos).then_inc(T["ld"], 16)
            sp.dma_start(sin[:, :], c_sin).then_inc(T["ld"], 16)
            sp.dma_start(window_f[:, :, :, :], c_window).then_inc(T["ld"], 16)

            def q_loads(b, p):
                cols = bass.ds(b * P, P)
                sp.dma_start(q_in[p][:, :, :], aq[:, :, cols]).then_inc(t_ld[p], 16)
                for to, of in halves:
                    sp.dma_start(q_sw[p][to, :, :], aq[of, :, cols]).then_inc(t_ld[p], 16)

            for b in range(2):
                q_loads(b, b)
            with sp.Fori(1, TT // 2) as i:
                for p in range(2):
                    sp.wait_ge(T["qrot"], 2 * i + p - 1)
                    q_loads(2 * i + p, p)

            for u in range(U_OUT + RAW, U_FFN2):
                load_unit(u, u % RAW, col_unit(w_out, (u - U_OUT) * P))
            with sp.Fori(0, GROUPS) as i:
                ffn_units(U_FFN2, w_ffn2_gate, w_ffn2_up, w_ffn2_down, i)

            for t in range(TT):
                sp.wait_ge(y_kept, 2 * t + 2)
                dst = y_prompt[0][t * P:(t + 1) * P, :] if t < 2 else y_sample[0][(t - 2) * P:(t - 1) * P, :]
                sp.dma_start(dst, y_out[t % 2][:, :]).then_inc(y_stored[t % 2], 16)
            for j in range(2):
                sp.wait_ge(y_stored[j], 16 * (TT // 2))

        @block.gpsimd
        def _(pool):
            pool.sem_inc(w_lo_ready, LO)

            def split_lo(unit, slot):
                pool.wait_ge(w_hi_ready, unit + 1)
                nc.gpsimd.tensor_tensor(w_lo[slot][:, :, :], w_raw[slot][:, :, :], w_hi[slot][:, :, :].bitcast(F32),
                                        ALU.subtract).then_inc(w_lo_ready, 1)

            early = U_OUT + RAW
            with pool.Fori(0, early // 3) as i:
                for j in range(3):
                    split_lo(3 * i + j, j)
            for u in range(early // 3 * 3, early):
                split_lo(u, u % 3)

            for h in range(GLA_HEADS):
                p = h % 2
                pool.wait_ge(g_ld[p], 80 * (h // 2 + 1))
                pool.wait_ge(G["ld_k"], 32 * (h + 1))
                nc.gpsimd.tensor_tensor(k_out[p][:, :], gk[:, :], k_out[p][:, :], ALU.mult).then_inc(G["ks"], 1)
                nc.gpsimd.tensor_tensor(k_in[p][:, :], gk[:, :], k_in[p][:, :], ALU.mult).then_inc(G["ke"], 1)
                if h == 0:
                    pool.wait_ge(G["s_zeroed"], 9)
                else:
                    pool.wait_ge(G["state"], 2 * h)
                pool.wait_ge(G["ke"], h + 1)
                for s, (a, b) in enumerate(zip(first_chunks, last_chunks)):
                    n = b - a
                    if s:
                        pool.wait_ge(G["decay"], 4 * h + 2)
                    nc.gpsimd.tensor_copy(gla_dec[0:DK, :, a + 1:b + 1],
                                          e_fw[p][0:DK, a * C + C - 1:b * C:C].unsqueeze(1).to_broadcast([DK, DV, n])
                                          ).then_inc(G["decay"], 1)
                    pool.wait_ge(G["decay"], 4 * h + 2 * s + 1)
                    nc.gpsimd.tensor_copy(gla_dec[DK:P, :, a:b],
                                          e_fw[p][DK:P, (a + 1) * C:b * C + 1:C].unsqueeze(1).to_broadcast([DK, DV, n])
                                          ).then_inc(G["decay"], 1)
                pool.wait_ge(G["decay"], 4 * h + 4)

            pool.wait_ge(T["keys"], 1)
            with pool.Fori(0, TT // 2) as i:
                for p in range(2):
                    b = 2 * i + p
                    cols = bass.ds(b * P, P)
                    pool.wait_ge(t_ld[p], 48 * i + 48)
                    nc.gpsimd.tensor_tensor(q_in[p][:, :, :], q_in[p][:, :, :],
                                            cos[:, cols].unsqueeze(1).to_broadcast([HD, HEADS, P]),
                                            ALU.mult).then_inc(T["qcos"], 1)
                    nc.gpsimd.tensor_tensor(q_sw[p][:, :, :], q_sw[p][:, :, :],
                                            sin[:, cols].unsqueeze(1).to_broadcast([HD, HEADS, P]),
                                            ALU.mult).then_inc(T["qsin"], 1)
                    pool.wait_ge(T["qcos"], b + 1)
                    pool.wait_ge(T["qsin"], b + 1)
                    pool.wait_ge(T["s"], HPG * b - 2 * HPG + S_FREE + 4)
                    nc.gpsimd.tensor_tensor(q_rot[p][:, :, :], q_in[p][:, :, :], q_sw[p][:, :, :],
                                            ALU.add).then_inc(T["qrot"], 1)

            rest = U_END - early
            with pool.Fori(0, rest // 3) as i:
                for j in range(3):
                    split_lo(early + 3 * i + j, (early + j) % 3)
            for u in range(early + rest // 3 * 3, U_END):
                split_lo(u, u % 3)

        @block.scalar
        def _(act):
            for j in range(3):
                act.sem_inc(in_stored[j], 16)
            act.sem_inc(G["e_stored"], 48)
            act.sem_inc(G["z"], GATE_FREE)
            act.sem_inc(T["p"], P_FREE)
            act.sem_inc(T["pT_act"], PT_FREE)
            act.sem_inc(T["o_kept"], OT_FREE)

            def split_hi(unit, slot):
                uses = 16 * (unit // RAW + 1) if isinstance(unit, int) else unit
                act.wait_ge(w_loaded[slot], uses)
                nc.scalar.activation(w_hi[slot][:, :, :], w_raw[slot][:, :, :], ACT.Copy).then_inc(w_hi_ready, 1)

            def loads_of(base, per, i, j):
                return 16 * (base // RAW + j // RAW + 1) + 16 * (per // RAW) * i

            def gained_hi(N, gain, c, k):
                c0, n = CHUNKS[c]
                nc.scalar.activation(h_hi[:, k, c0:c0 + n], xT[:, k, c0:c0 + n], ACT.Copy,
                                     scale=gains[:, gain, k:k + 1]).then_inc(N["hi"], 1)

            def squares(N, c, k, idx, ring):
                c0, n = CHUNKS[c]
                if idx >= ring:
                    act.wait_ge(N["sum"], idx - ring + 1)
                nc.scalar.activation(square[idx % ring][:, 0:n], xT[:, k, c0:c0 + n], ACT.Square
                                     ).then_inc(N["square"], 1)

            def roots(N):
                for c, (c0, n) in enumerate(CHUNKS):
                    act.wait_ge(N["mean"], c + 1)
                    nc.scalar.activation(rstd[:, c0:c0 + n], rstd[:, c0:c0 + n], ACT.Sqrt).then_inc(N["sqrt"], 1)

            def ffn_end(A, N, gain, final=False):
                done = DN_FREE + 24 * (GROUPS - 1)
                for c in range(NCH):
                    for k in range(KT):
                        act.wait_ge(A["dn_added"], done + KT * c + k + 1)
                        if not final:
                            gained_hi(N, gain, c, k)
                    if c:
                        for k in range(KT):
                            squares(N, c - 1, k, KT * (c - 1) + k, 2)
                for k in range(KT):
                    squares(N, NCH - 1, k, KT * (NCH - 1) + k, 2)
                roots(N)

            def ffn_body(A, base, i, last=False):
                def split(j):
                    act.wait_ge(w_loaded[j % RAW], loads_of(base, 6, i, j))
                    nc.scalar.activation(w_hi[j % SPLIT][:, :, :], w_raw[j % RAW][:, :, :],
                                         ACT.Copy).then_inc(w_hi_ready, 1)

                act.wait_ge(A["dn_done"], DN_USED + 24 * i)
                split(1)
                split(2)
                for s in range(6):
                    t, (c0, n) = s // NCH, CHUNKS[s % NCH]
                    if s % NCH == 2:
                        act.wait_ge(A["gate_used"], 2 * i + t + 1)
                        split(3 + 2 * t)
                    act.wait_ge(A["gate_rs"], 6 * i + s + 1)
                    nc.scalar.activation(silu[s % 2][:, 0:n], scaled_g[s % 2][:, 0:n], ACT.Silu).then_inc(A["silu"], 1)
                    act.wait_ge(A["prod"], 6 * i + s + 1)
                    nc.scalar.activation(hid_hi[:, t, c0:c0 + n], prod[s % 2][:, 0:n],
                                         ACT.Copy).then_inc(A["hid_hi"], 1)
                    if s % NCH == 2 and not (last and t == 1):
                        act.wait_ge(A["gu_done"], 6 * i + s + 1)
                        split(4 + 2 * t)

            for c, (c0, n) in enumerate(CHUNKS):
                for t in range(c0 // P, (c0 + n) // P):
                    act.wait_ge(x_turned, 2 * t + 1)
                    nc.scalar.copy(xT[:, 0:4, t * P:(t + 1) * P],
                                   ps[:, 4 + 2 * (t % 2), :].rearrange("p (k n) -> p k n", k=4)).then_inc(x_kept_act, 1)
                act.wait_ge(x_kept_act, (c0 + n) // P)
                act.wait_ge(x_kept_dve, (c0 + n) // P)
                if c == 0:
                    act.wait_ge(ld_const, 16 * N_CONST_LD)
                for k in range(KT):
                    gained_hi(N1, 0, c, k)
                if c == 0:
                    act.wait_ge(w_loaded[0], 16)
                    nc.scalar.activation(w_hi[0][:, :, :], w_raw[0][:, :, :], ACT.Copy).then_inc(w_hi_ready, 1)
                else:
                    for k in range(KT):
                        squares(N1, c - 1, k, KT * (c - 1) + k, 2)
            for k in range(KT):
                squares(N1, NCH - 1, k, KT * (NCH - 1) + k, 2)
            roots(N1)
            with act.Fori(0, GROUPS) as i:
                ffn_body(A1, 0, i)
            ffn_end(A1, NM, 1)

            act.dma_start(reset[:, :], c_reset).then_inc(G["ld_reset"], 16)
            act.wait_ge(G["zeroed"], 1)

            def split_ahead(i, j, w):
                act.wait_ge(in_done, IN_USED + NCH * w - NCH)
                act.wait_ge(w_loaded[(j + 1) % RAW], loads_of(U_IN, 3, i, j + 1))
                nc.scalar.activation(w_hi[(j + 1) % SPLIT][:, :, :], w_raw[(j + 1) % RAW][:, :, :],
                                     ACT.Copy).then_inc(w_hi_ready, 1)

            def store(j, w):
                act.wait_ge(in_moved, IN_FREE + NCH * w + NCH)
                act.dma_start(proj[bass.ds((w - 1) * P, P), :], stage[j][:, :]).then_inc(in_stored[j], 16)

            def load_decay(h):
                act.wait_ge(G["gate"], NCH * h + NCH)
                for half, (wd, bd) in enumerate(((w_gla_decay_fwd, b_gla_decay_fwd), (w_gla_decay_bwd, b_gla_decay_bwd))):
                    act.dma_start(w_dec[2 * RANK:2 * RANK + 1, half * DK:(half + 1) * DK],
                                  bd[:, bass.ds(h * DK, DK)]).then_inc(G["w_ld"], 16)
                    act.dma_start(w_dec[half * RANK:(half + 1) * RANK, half * DK:(half + 1) * DK],
                                  wd[0][:, bass.ds(h * DK, DK)]).then_inc(G["w_ld"], 16)

            def log_gate(h):
                act.wait_ge(G["e_stored"], 48 * h + 48)
                for c, (c0, n) in enumerate(CHUNKS):
                    act.wait_ge(G["gate"], NCH * h + NCH + c + 1)
                    nc.scalar.activation(gla_z[:, c0:c0 + n], ps[:, c, 0:n], ACT.Copy).then_inc(G["z"], 1)
                act.wait_ge(G["z"], GATE_FREE + NCH * h + NCH)
                nc.scalar.activation(gla_t[:, :], gla_z[:, :], ACT.Abs).then_inc(G["abs"], 1)
                act.wait_ge(G["abs"], h + 1)
                nc.scalar.activation(gla_t[:, :], gla_t[:, :], ACT.Exp, scale=-1.0).then_inc(G["exp"], 1)
                act.wait_ge(G["exp"], h + 1)
                nc.scalar.activation(gla_t[:, :], gla_t[:, :], ACT.Ln, bias=1.0).then_inc(G["ln"], 1)

            def decays(h):
                act.wait_ge(G["scan"], 2 * h + 2)
                nc.scalar.activation(gla_t[:, :], gla_b[:, :], ACT.Exp, scale=1.0 / GATE_NORM).then_inc(G["eb"], 1)
                act.wait_ge(G["diff"], 2 * h + 2)
                nc.scalar.activation(gla_z[:, :], gla_z[:, :], ACT.Exp, scale=1.0 / GATE_NORM).then_inc(G["es"], 1)
                act.wait_ge(G["eb"], h + 1)
                nc.scalar.activation(gla_b[:, :], gla_b[:, :], ACT.Exp, scale=-1.0 / GATE_NORM).then_inc(G["enb"], 1)
                act.wait_ge(G["enb"], h + 1)
                act.wait_ge(G["es"], h + 1)
                for e, decay in enumerate((gla_t, gla_b, gla_z)):
                    act.dma_start(proj[bass.ds(h * 3 * P + (ROW_E + e * P), P), :], decay[:, :]
                                  ).then_inc(G["e_stored"], 16)

            split_ahead(0, 0, 0)
            with act.Fori(0, GLA_HEADS) as i:
                load_decay(i)
                split_ahead(i, 1, 3 * i + 1)
                store(0, 3 * i + 1)
                split_ahead(i, 2, 3 * i + 2)
                log_gate(i)
                store(1, 3 * i + 2)
                split_ahead(i, 3, 3 * i + 3)
                decays(i)
                store(2, 3 * i + 3)
            with act.Fori(GLA_HEADS, IN_TILES // 3) as i:
                for j in range(3):
                    split_ahead(i, j + 1, 3 * i + (j + 1))
                    store(j, 3 * i + (j + 1))
            act.wait_ge(in_done, IN_USED + NCH * IN_TILES)
            split_hi(U_OUT + 1, (U_OUT + 1) % SPLIT)
            act.wait_ge(in_done, IN_USED + NCH * (IN_TILES + 1))
            split_hi(U_OUT + 2, (U_OUT + 2) % SPLIT)

            def turned(h, name, done, to):
                for c, (c0, n) in enumerate(CHUNKS):
                    act.wait_ge(G[name], NCH * h + c + 1)
                    nc.scalar.copy(to[:, c0 // P:(c0 + n) // P, :],
                                   ps[:, 4 + c, 0:n].rearrange("p (t d) -> p t d", d=P)).then_inc(G[done], 1)

            turned(0, "vT", "vN", gla_vn[0])
            turned(0, "kT", "kN", gla_kn)
            act.wait_ge(G["s_zeroed"], 9)
            for h in range(GLA_HEADS):
                if h >= 2:
                    act.wait_ge(G["o"], NCH * (h - 1))
                act.wait_ge(G["u"], h + 1)
                for start, parity in ((0, 0), (1, 1)):
                    for a, b in zip(first_chunks, last_chunks):
                        n = len(range(a + start, b, 2))
                        col = u_col(a + start)
                        nc.scalar.copy(gla_s[h % 2][0:DK, :, a + start + 1:b + 1:2],
                                       psf[0:DK, col:col + n * DV].rearrange("p (n d) -> p d n", d=DV)
                                       ).then_inc(G["u_fw"], 1)
                if h + 1 < GLA_HEADS:
                    turned(h + 1, "vT", "vN", gla_vn[(h + 1) % 2])
                    turned(h + 1, "kT", "kN", gla_kn)
                for c, (c0, n) in enumerate(CHUNKS):
                    act.wait_ge(G["o"], NCH * h + c + 1)
                    nc.scalar.copy(o_raw[:, 4 + h, c0:c0 + n], ps[:, O_BANKS[c], 0:n]).then_inc(G["o_kept"], 1)
            act.wait_ge(G["o_kept"], NCH * GLA_HEADS)
            act.wait_ge(gn["ld"], 16 * GLA_HEADS)
            for h in range(GLA_HEADS):
                nc.scalar.activation(gg[:, h, :], gg[:, h, :], ACT.Silu).then_inc(gn["silu"], 1)
            for h in range(GLA_HEADS):
                for c, (c0, n) in enumerate(CHUNKS):
                    r = NCH * h + c
                    if h:
                        act.wait_ge(gn["sum"], r - NCH + 1)
                    nc.scalar.activation(gsq[c][:, 0:n], o_raw[:, 4 + h, c0:c0 + n],
                                         ACT.Square).then_inc(gn["square"], 1)
                for c, (c0, n) in enumerate(CHUNKS):
                    act.wait_ge(gn["mean"], NCH * h + c + 1)
                    nc.scalar.activation(grs[c][:, 0:n], grs[c][:, 0:n], ACT.Sqrt).then_inc(gn["sqrt"], 1)

            for j in range(3):
                act.wait_ge(T["vT"], j + 1)
                c0, n = CHUNKS[j]
                nc.scalar.copy(vN[:, 1 + c0 // P:1 + (c0 + n) // P, :],
                               ps[:, 4 + j, 0:n].rearrange("p (t d) -> p t d", d=P)).then_inc(T["vN"], 1)
            act.wait_ge(T["ld"], 7 * 16)
            nc.scalar.copy(window[:, :, :, :], window_f[:, :, :, :]).then_inc(T["window"], 1)
            act.wait_ge(T["window"], 1)
            act.wait_ge(T["keys"], 1)
            act.wait_ge(T["vN"], 3)

            def attend(u, i, r, first, drain):
                st = stats[r % 4]
                if not drain:
                    act.wait_ge(T["negm"], u + 1)
                    for e in range(2):
                        nc.scalar.activation(probs[r % 4][:, e, :], ps[:, 2 * (r % 2) + e, 0:3 * P], ACT.Exp,
                                             bias=st[:, NEGM, e:e + 1], scale=HD ** -0.5,
                                             accum_out=st[:, SUM, e:e + 1]).then_inc(T["p"], 1)
                    act.wait_ge(T["dsink"], u + 1)
                    nc.scalar.activation(st[:, ESINK, :], st[:, DSINK, :], ACT.Exp).then_inc(T["es"], 1)
                if not (first and r < 2) and not (drain and r >= 2):
                    act.wait_ge(T["turned"], u - 1)
                    nc.scalar.copy(probsT[:, 0, :, :],
                                   ps[:, 4, 0:3 * P].rearrange("p (j q) -> p j q", j=3)).then_inc(T["pT_act"], 1)
                if not (first and r < 4):
                    act.wait_ge(T["oT"], u - 3)
                    cols = bass.ds((2 * i + (r - 4) // 4) * P, P)
                    nc.scalar.copy(o_raw[:, (r - 4) % 4, cols], ps[:, 7, 0:P]).then_inc(T["o_kept"], 1)

            for r in range(8):
                attend(r, 0, r, True, False)
            with act.Fori(1, TT // 2) as i:
                for r in range(8):
                    attend(8 * i + r, i, r, False, False)
            for r in range(4):
                attend(TT // 2 * 8 + r, TT // 2, r, False, True)

            act.wait_ge(T["o_kept"], OT_FREE + HPG * TT)
            act.wait_ge(T["s"], S_FREE + HPG * TT)
            for c, (c0, n) in enumerate(CHUNKS):
                for k in range(KT):
                    nc.scalar.activation(h_hi[:, k, c0:c0 + n], o_raw[:, k, c0:c0 + n], ACT.Copy).then_inc(o_hi, 1)
            for n in range(KT):
                if n < KT - 2:
                    act.wait_ge(out_done, NCH * (n + 1))
                    split_hi(U_OUT + RAW + n, (U_OUT + RAW + n) % SPLIT)
                for c in range(NCH):
                    act.wait_ge(out_added, IN_FREE + NCH * n + c + 1)
                    if n == KT - 1:
                        act.wait_ge(out_done, NCH * n + c + 1)
                        for k in range(KT):
                            gained_hi(N2, 2, c, k)
                    squares(N2, c, n, NCH * n + c, 3)
            roots(N2)
            with act.Fori(0, GROUPS - 1) as i:
                ffn_body(A2, U_FFN2, i)
            ffn_body(A2, U_FFN2, GROUPS - 1, last=True)
            ffn_end(A2, NF, 3, final=True)
            for t in range(TT):
                for half in range(2):
                    act.wait_ge(y_turned, 2 * t + half + 1)
                    if t >= 2 and half == 0:
                        act.wait_ge(y_stored[t % 2], 16 * (t // 2))
                    nc.scalar.copy(y_out[t % 2][:, half * 512:(half + 1) * 512],
                                   ps[:, 4 + 2 * (t % 2) + half, :]).then_inc(y_kept, 1)

        @block.vector
        def _(dve):
            v = nc.vector
            for A in (A1, A2):
                dve.sem_inc(A["up_rs"], GU_FREE)
                dve.sem_inc(A["dn_added"], DN_FREE)
            dve.sem_inc(in_moved, IN_FREE)
            dve.sem_inc(out_added, IN_FREE)
            dve.sem_inc(T["pT_dve"], PT_FREE)
            dve.sem_inc(T["o_nat"], ON_FREE)
            v.memset(ones[:, :], 1.0).then_inc(const_ones, 1)
            dve.wait_ge(ld_const, 16 * N_CONST_LD)
            v.tensor_copy(ident_bf[:, :], ident[:, :]).then_inc(const_bf, 1)
            v.tensor_scalar(neg_sinks[:, :], sinks[:, :], -1.0, None, ALU.mult).then_inc(const_neg, 1)

            def gained_lo(N, gain, c, k, idx):
                c0, n = CHUNKS[c]
                dve.wait_ge(N["hi"], idx + 1)
                v.scalar_tensor_tensor(out=h_lo[:, k, c0:c0 + n], in0=xT[:, k, c0:c0 + n], scalar=gains[:, gain, k:k + 1],
                                       in1=h_hi[:, k, c0:c0 + n].bitcast(F32), op0=ALU.mult, op1=ALU.subtract
                                       ).then_inc(N["lo"], 1)

            def mean(N, c, bank):
                c0, n = CHUNKS[c]
                dve.wait_ge(N["sum"], KT * (c + 1) if N is not N2 else KT * NCH)
                v.tensor_scalar(rstd[:, c0:c0 + n], ps[:, bank, 0:n], 1.0 / D_MODEL, EPS, ALU.mult, ALU.add
                                ).then_inc(N["mean"], 1)

            def invert(N, c):
                c0, n = CHUNKS[c]
                dve.wait_ge(N["sqrt"], c + 1)
                v.reciprocal(rstd[:, c0:c0 + n], rstd[:, c0:c0 + n]).then_inc(N["rstd"], 1)

            for c, (c0, n) in enumerate(CHUNKS):
                for t in range(c0 // P, (c0 + n) // P):
                    dve.wait_ge(x_turned, 2 * t + 2)
                    v.tensor_copy(xT[:, 4:8, t * P:(t + 1) * P],
                                  ps[:, 5 + 2 * (t % 2), :].rearrange("p (k n) -> p k n", k=4)).then_inc(x_kept_dve, 1)
                for k in range(KT):
                    gained_lo(N1, 0, c, k, KT * c + k)
                if c:
                    mean(N1, c - 1, SUMS[c - 1])
            mean(N1, NCH - 1, SUMS[NCH - 1])
            for c in range(NCH):
                invert(N1, c)

            def ffn_body(A, N, i, last=None):
                for s in range(6):
                    t, c = s // NCH, s % NCH
                    c0, n = CHUNKS[c]
                    b = s % 2
                    r = rstd[:, c0:c0 + n]
                    if t == 0:
                        dve.wait_ge(N["rstd"], c + 1)
                    dve.wait_ge(A["gu_done"], 6 * i + s + 1)
                    v.tensor_tensor(scaled_g[b][:, 0:n], r, ps[:, GU + 2 * b, 0:n], ALU.mult).then_inc(A["gate_rs"], 1)
                    v.tensor_tensor(scaled_u[b][:, 0:n], r, ps[:, GU + 2 * b + 1, 0:n], ALU.mult
                                    ).then_inc(A["up_rs"], 1)
                    dve.wait_ge(A["silu"], 6 * i + s + 1)
                    dve.wait_ge(A["up_rs"], GU_FREE + 6 * i + s + 1)
                    v.tensor_tensor(prod[b][:, 0:n], silu[b][:, 0:n], scaled_u[b][:, 0:n], ALU.mult
                                    ).then_inc(A["prod"], 1)
                    dve.wait_ge(A["hid_hi"], 6 * i + s + 1)
                    v.tensor_tensor(hid_lo[:, t, c0:c0 + n], prod[b][:, 0:n], hid_hi[:, t, c0:c0 + n].bitcast(F32),
                                    ALU.subtract).then_inc(A["hid_lo"], 1)
                for c, (c0, n) in enumerate(CHUNKS):
                    for k in range(KT):
                        m = KT * c + k
                        dve.wait_ge(A["dn_done"], DN_USED + 24 * i + m + 1)
                        v.scalar_tensor_tensor(out=xT[:, k, c0:c0 + n], in0=ps[:, DN + m % 4, 0:n], scalar=0.5,
                                               in1=xT[:, k, c0:c0 + n], op0=ALU.mult,
                                               op1=ALU.add).then_inc(A["dn_added"], 1)
                    if last:
                        last(c)

            def ffn(A, N, last):
                with dve.Fori(0, GROUPS - 1) as i:
                    ffn_body(A, N, i)
                ffn_body(A, N, GROUPS - 1, last)

            def to_mix(c):
                for k in range(KT):
                    gained_lo(NM, 1, c, k, KT * c + k)
                if c:
                    mean(NM, c - 1, SUMS[c - 1])

            ffn(A1, N1, to_mix)
            mean(NM, NCH - 1, SUMS[NCH - 1])
            for c in range(NCH):
                invert(NM, c)

            dve.wait_ge(NM["sum"], KT * NCH)
            v.memset(w_dec[:, :], 0.0).then_inc(G["zeroed"], 1)
            dve.wait_ge(A1["dn_done"], DN_USED + 24 * GROUPS)
            v.memset(rT[2 * RANK:2 * RANK + 1, :], 1.0).then_inc(G["ones"], 1)
            for c, (c0, n) in enumerate(CHUNKS):
                dve.wait_ge(in_done, IN_USED + c + 1)
                dve.wait_ge(NM["rstd"], c + 1)
                v.tensor_tensor(rT[0:2 * RANK, c0:c0 + n], rstd[0:2 * RANK, c0:c0 + n], ps[0:2 * RANK, 4 + c, 0:n], ALU.mult
                                ).then_inc(in_moved, 1)

            def in_unit(i, j, w):
                dve.wait_ge(in_stored[j], 16 + 16 * i)
                for c, (c0, n) in enumerate(CHUNKS):
                    dve.wait_ge(in_done, IN_USED + NCH * w + c + 1)
                    v.tensor_tensor(stage[j][:, c0:c0 + n], rstd[:, c0:c0 + n], ps[:, 4 + c, 0:n],
                                    ALU.mult).then_inc(in_moved, 1)

            fw, bw = slice(0, DK), slice(DK, P)

            def cumulate(h):
                dve.wait_ge(G["ln"], h + 1)
                v.scalar_tensor_tensor(out=gla_z[:, :], in0=gla_z[:, :], scalar=0.0, in1=gla_t[:, :],
                                       op0=ALU.min, op1=ALU.subtract).then_inc(G["log"], 1)
                dve.wait_ge(G["log"], h + 1)
                v.tensor_tensor_scan(gla_b[fw, :], reset[fw, :], gla_z[fw, :], 0.0, ALU.mult, ALU.add
                                     ).then_inc(G["scan"], 1)
                v.tensor_tensor_scan(gla_b[bw, ::-1], reset[bw, ::-1], gla_z[bw, ::-1], 0.0, ALU.mult, ALU.add
                                     ).then_inc(G["scan"], 1)
                dve.wait_ge(G["scan"], 2 * h + 2)
                for rows, edge in ((fw, C - 1), (bw, 0)):
                    bc = gla_b[rows, :].rearrange("p (n c) -> p n c", c=C)
                    v.tensor_tensor(gla_z[rows, :].rearrange("p (n c) -> p n c", c=C),
                                    bc[:, :, edge:edge + 1].to_broadcast([DK, TOK // C, C]), bc,
                                    ALU.subtract).then_inc(G["diff"], 1)

            dve.wait_ge(G["ld_reset"], 16)
            with dve.Fori(0, GLA_HEADS) as i:
                in_unit(i, 0, 3 * i + 1)
                in_unit(i, 1, 3 * i + 2)
                cumulate(i)
                in_unit(i, 2, 3 * i + 3)
            with dve.Fori(GLA_HEADS, IN_TILES // 3) as i:
                for j in range(3):
                    in_unit(i, j, 3 * i + (j + 1))

            for j in range(3):
                dve.wait_ge(in_stored[j], 16 + 16 * IN_TILES // 3)
            dve.wait_ge(in_done, IN_USED + NCH * (IN_TILES + 1))
            for a, b in zip(first_chunks, last_chunks):
                for t in gla_s:
                    v.memset(t[fw, :, a:a + 1], 0.0).then_inc(G["s_zeroed"], 1)
                    v.memset(t[bw, :, b:b + 1], 0.0).then_inc(G["s_zeroed"], 1)
            v.memset(gla_dec[:, :, :], 0.0).then_inc(G["s_zeroed"], 1)
            dve.wait_ge(G["ld_masks"], 16)

            def query(h):
                p = h % 2
                dve.wait_ge(g_ld[p], 80 * (h // 2 + 1))
                v.scalar_tensor_tensor(out=gq[p][:, :], in0=gq[p][:, :], scalar=DK ** -0.5, in1=e_fw[p][:, :],
                                       op0=ALU.mult, op1=ALU.mult).then_inc(G["qe"], 1)

            def mask(h):
                a = gla_a[h % 2]
                for c, (c0, n) in enumerate(CHUNKS):
                    t0, t1 = c0 // P, (c0 + n) // P
                    dve.wait_ge(G["scores"], NCH * h + c + 1)
                    back = ps[:, 1, 0:n].rearrange("p (t i) -> p t i", i=P)
                    for d, out, name in ((0, a[:, t0:t1, :], "masked_f"), (1, back, "masked_b")):
                        v.tensor_tensor(out, ps[:, d, 0:n].rearrange("p (t i) -> p t i", i=P),
                                        masks[:, d:d + 1, :].to_broadcast([P, t1 - t0, P]), ALU.mult
                                        ).then_inc(G[name], 1)
                    dve.wait_ge(G["masked_f"], NCH * h + c + 1)
                    dve.wait_ge(G["masked_b"], NCH * h + c + 1)
                    v.tensor_tensor(a[:, t0:t1, :], a[:, t0:t1, :], back, ALU.add).then_inc(G["masked"], 1)

            query(0)
            mask(0)
            for h in range(GLA_HEADS):
                s = gla_s[h % 2]
                if h + 1 < GLA_HEADS:
                    query(h + 1)
                if h >= 2:
                    dve.wait_ge(G["o"], NCH * (h - 1))
                dve.wait_ge(G["u"], h + 1)
                for start in range(2):
                    for a, b in zip(first_chunks, last_chunks):
                        n0 = a + 1 + start
                        n = len(range(n0, b + 1, 2))
                        col = u_col(n0)
                        v.tensor_copy(s[bw, :, n0 - 1:b:2], psf[bw, col:col + n * DV].rearrange("p (n d) -> p d n", d=DV)
                                      ).then_inc(G["u_bw"], 1)
                dve.wait_ge(G["decay"], 4 * h + 4)
                dve.wait_ge(G["u_bw"], 4 * h + 4)
                flat, dec = s[:, :, :].rearrange("p d n -> p (d n)"), gla_dec[:, :, :].rearrange("p d n -> p (d n)")
                v.tensor_tensor_scan(flat[bw, ::-1], dec[bw, ::-1], flat[bw, ::-1], 0.0, ALU.mult, ALU.add
                                     ).then_inc(G["state"], 1)
                dve.wait_ge(G["u_fw"], 4 * h + 4)
                v.tensor_tensor_scan(flat[fw, :], dec[fw, :], flat[fw, :], 0.0, ALU.mult, ALU.add
                                     ).then_inc(G["state"], 1)
                if h + 1 < GLA_HEADS:
                    mask(h + 1)
            dve.wait_ge(gn["silu"], GLA_HEADS)
            for h in range(GLA_HEADS):
                for c, (c0, n) in enumerate(CHUNKS):
                    dve.wait_ge(gn["sum"], NCH * h + c + 1)
                    v.tensor_scalar(grs[c][:, 0:n], ps[:, c, 0:n], 1.0 / DV, EPS, ALU.mult, ALU.add
                                    ).then_inc(gn["mean"], 1)
                for c, (c0, n) in enumerate(CHUNKS):
                    r = NCH * h + c
                    o = o_raw[:, 4 + h, c0:c0 + n]
                    dve.wait_ge(gn["sqrt"], r + 1)
                    v.reciprocal(grs[c][:, 0:n], grs[c][:, 0:n]).then_inc(gn["rstd"], 1)
                    dve.wait_ge(gn["rstd"], r + 1)
                    v.scalar_tensor_tensor(out=o, in0=o, scalar=gla_gain[:, 0:1], in1=grs[c][:, 0:n],
                                           op0=ALU.mult, op1=ALU.mult).then_inc(gn["scaled"], 1)
                    dve.wait_ge(gn["scaled"], r + 1)
                    v.tensor_tensor(o, o, gg[:, h, c0:c0 + n], ALU.mult).then_inc(gn["gated"], 1)

            dve.wait_ge(T["ld"], 7 * 16)
            v.memset(kT[:, :, 0:P], 0.0).then_inc(T["pads"], 1)
            v.memset(kT[:, :, P + TOK:], 0.0).then_inc(T["pads"], 1)
            v.memset(vN[:, 0, :], 0.0).then_inc(T["pads"], 1)
            v.memset(vN[:, TT + 1, :], 0.0).then_inc(T["pads"], 1)
            keys = kT[:, :, P:P + TOK]
            v.tensor_tensor(keys, keys, cos[:, :].unsqueeze(1).to_broadcast([HD, KV, TOK]), ALU.mult
                            ).then_inc(T["cosd"], 1)
            v.tensor_tensor(k_sw[:, :, :], k_sw[:, :, :], sin[:, :].unsqueeze(1).to_broadcast([HD, KV, TOK]), ALU.mult
                            ).then_inc(T["sind"], 1)
            dve.wait_ge(T["cosd"], 1)
            dve.wait_ge(T["sind"], 1)
            v.tensor_tensor(keys, keys, k_sw[:, :, :], ALU.add).then_inc(T["keys"], 1)

            def attend(u, r, first, drain):
                st = stats[r % 4]
                t = r % 4
                if not drain:
                    dve.wait_ge(T["s"], S_FREE + u + 1)
                    v.reduce_max(st[:, MX, :], ps[:, 2 * (r % 2):2 * (r % 2) + 2, 0:3 * P], AX.X).then_inc(T["max"], 1)
                    dve.wait_ge(T["max"], u + 1)
                    v.scalar_tensor_tensor(out=st[:, NEGM, :], in0=st[:, MX, :], scalar=-HD ** -0.5,
                                           in1=neg_sinks[:, 2 * t:2 * t + 2], op0=ALU.mult, op1=ALU.min
                                           ).then_inc(T["negm"], 1)
                    dve.wait_ge(T["negm"], u + 1)
                    v.tensor_tensor(st[:, DSINK, :], st[:, NEGM, :], sinks[:, 2 * t:2 * t + 2], ALU.add
                                    ).then_inc(T["dsink"], 1)
                if not (first and r < 3) and not (drain and r >= 3):
                    old = stats[(r - 3) % 4]
                    dve.wait_ge(T["pv"], u - 2)
                    if not (first and r < 5):
                        dve.wait_ge(T["oT"], u - 4)
                    for e in range(2):
                        v.tensor_scalar(o_nat[(r - 3) % 2][:, e * HD:(e + 1) * HD], ps[:, 6, e * HD:(e + 1) * HD],
                                        old[:, RDEN, e:e + 1], None, ALU.mult).then_inc(T["o_nat"], 1)
                if not (first and r < 2) and not (drain and r >= 2):
                    dve.wait_ge(T["turned"], u - 1)
                    v.tensor_copy(probsT[:, 1, :, :],
                                  ps[:, 5, 0:3 * P].rearrange("p (j q) -> p j q", j=3)).then_inc(T["pT_dve"], 1)
                if not (first and r < 1) and not (drain and r >= 1):
                    new = stats[(r - 1) % 4]
                    dve.wait_ge(T["es"], u)
                    v.tensor_tensor(new[:, RDEN, :], new[:, SUM, :], new[:, ESINK, :], ALU.add).then_inc(T["den"], 1)
                    dve.wait_ge(T["den"], u)
                    v.reciprocal(new[:, RDEN, :], new[:, RDEN, :]).then_inc(T["rden"], 1)

            dve.wait_ge(const_neg, 1)
            for r in range(8):
                attend(r, r, True, False)
            with dve.Fori(1, TT // 2) as i:
                for r in range(8):
                    attend(8 * i + r, r, False, False)
            for r in range(4):
                attend(TT // 2 * 8 + r, r, False, True)

            for c, (c0, n) in enumerate(CHUNKS):
                for k in range(KT):
                    dve.wait_ge(o_hi, KT * c + k + 1)
                    v.tensor_tensor(h_lo[:, k, c0:c0 + n], o_raw[:, k, c0:c0 + n], h_hi[:, k, c0:c0 + n].bitcast(F32),
                                    ALU.subtract).then_inc(o_lo, 1)

            def out_unit(n, first=False):
                for c, (c0, w) in enumerate(CHUNKS):
                    dve.wait_ge(out_done, NCH * n + c + 1)
                    v.tensor_tensor(xT[:, n, c0:c0 + w], ps[:, c, 0:w], xT[:, n, c0:c0 + w], ALU.add
                                    ).then_inc(out_added, 1)
            for n in range(KT):
                out_unit(n)
            for c in range(NCH):
                for k in range(KT):
                    gained_lo(N2, 2, c, k, KT * c + k)
            for c in range(NCH):
                mean(N2, c, 4 + c)
            for c in range(NCH):
                invert(N2, c)
            ffn(A2, N2, lambda c: mean(NF, c - 1, SUMS[c - 1]) if c else None)
            mean(NF, NCH - 1, SUMS[NCH - 1])
            for c, (c0, n) in enumerate(CHUNKS):
                invert(NF, c)
                dve.wait_ge(NF["rstd"], c + 1)
                for t in range(c0 // P, (c0 + n) // P):
                    cols = slice(t * P, (t + 1) * P)
                    if t >= 2:
                        dve.wait_ge(y_turned, 2 * t - 2)
                    for k in range(KT):
                        v.scalar_tensor_tensor(out=normed[t % 2][:, k, :], in0=xT[:, k, cols],
                                               scalar=gains[:, 3, k:k + 1], in1=rstd[:, cols],
                                               op0=ALU.mult, op1=ALU.mult).then_inc(y_scaled, 1)

        @block.tensor
        def _(pe):
            mm = nc.tensor.matmul
            for A in (A1, A2):
                pe.sem_inc(A["dn_done"], DN_USED)
            pe.sem_inc(in_done, IN_USED)
            pe.sem_inc(G["gate"], NCH)
            pe.sem_inc(T["s"], S_FREE)

            def mm3(out, wslot, wk, rhs_hi, rhs_lo, first, last, width=P):
                hi, lo = w_hi[wslot][:, wk, 0:width], w_lo[wslot][:, wk, 0:width]
                mm(out, hi, rhs_hi, start=first, stop=False)
                mm(out, hi, rhs_lo, start=False, stop=False)
                return mm(out, lo, rhs_hi, start=False, stop=last)

            def project(bank, c, wslot, width=P):
                c0, n = CHUNKS[c]
                for k in range(KT):
                    last = mm3(ps[0:width, bank, 0:n], wslot, k, h_hi[:, k, c0:c0 + n], h_lo[:, k, c0:c0 + n],
                               k == 0, k == KT - 1, width)
                return last

            def sums(N, c, bank):
                if c == 2:
                    pe.wait_ge(N["mean"], 1)
                for k in range(KT):
                    pe.wait_ge(N["square"], KT * c + k + 1)
                    mm(ps[:, bank, 0:CHUNKS[c][1]], ones[:, :], square[(KT * c + k) % 2][:, 0:CHUNKS[c][1]],
                       start=(k == 0), stop=(k == KT - 1)).then_inc(N["sum"], 1)

            def h_ready(N, c):
                pe.wait_ge(N["lo"], KT * (c + 1))

            def ffn_body(A, N, base, i, last=None):
                for s in range(6):
                    t, c = s // NCH, s % NCH
                    g_slot, u_slot = 2 * t % SPLIT, (2 * t + 1) % SPLIT
                    if t == 0:
                        h_ready(N, c)
                    if s == 1:
                        pe.wait_ge(N["mean"], NCH)
                    if c == 0:
                        pe.wait_ge(w_lo_ready, LO + base + 6 * i + 2 * t + 1)
                    pe.wait_ge(A["up_rs"], 6 * i + s + 1)
                    done = project(GU + 2 * (s % 2), c, g_slot)
                    if c == NCH - 1:
                        done.then_inc(A["gate_used"], 1)
                    if c == 0:
                        pe.wait_ge(w_lo_ready, LO + base + 6 * i + 2 * t + 2)
                    project(GU + 2 * (s % 2) + 1, c, u_slot).then_inc(A["gu_done"], 1)
                pe.wait_ge(w_lo_ready, LO + base + 6 * i + 6)
                for c, (c0, n) in enumerate(CHUNKS):
                    pe.wait_ge(A["hid_lo"], 6 * i + NCH + c + 1)
                    for k in range(KT):
                        m = KT * c + k
                        pe.wait_ge(A["dn_added"], 24 * i + m + 1)
                        for t in range(2):
                            done = mm3(ps[:, DN + m % 4, 0:n], (4 + t) % SPLIT, k, hid_hi[:, t, c0:c0 + n],
                                       hid_lo[:, t, c0:c0 + n], t == 0, t == 1)
                        done.then_inc(A["dn_done"], 1)
                    if last and c:
                        sums(last, c - 1, SUMS[c - 1])
                if last:
                    sums(last, NCH - 1, SUMS[NCH - 1])

            def ffn(A, N, base, after):
                with pe.Fori(0, GROUPS - 1) as i:
                    ffn_body(A, N, base, i)
                ffn_body(A, N, base, GROUPS - 1, after)

            pe.wait_ge(ld_const, 16 * N_CONST_LD)
            pe.wait_ge(const_ones, 1)
            for c, (c0, n) in enumerate(CHUNKS):
                for t in range(c0 // P, (c0 + n) // P):
                    pe.wait_ge(x_loaded[t % 4], 16 * (t // 4 + 1))
                    if t >= 2:
                        pe.wait_ge(x_kept_act, t - 1)
                        pe.wait_ge(x_kept_dve, t - 1)
                    for half in range(2):
                        for k in range(4):
                            last = nc.tensor.transpose(ps[:, 4 + 2 * (t % 2) + half, k * P:(k + 1) * P],
                                                       x_in[t % 4][:, (4 * half + k) * P:(4 * half + k + 1) * P],
                                                       ident[:, :])
                        last.then_inc(x_turned, 1)
                if c:
                    sums(N1, c - 1, SUMS[c - 1])
            sums(N1, NCH - 1, SUMS[NCH - 1])
            ffn(A1, N1, 0, NM)

            def in_unit(slot, w, width=P):
                pe.wait_ge(w_lo_ready, LO + U_IN + w + 1)
                for c in range(NCH):
                    h_ready(NM, c)
                    pe.wait_ge(in_moved, NCH * w + c + 1)
                    project(4 + c, c, slot, width).then_inc(in_done, 1)

            def gates(h):
                pe.wait_ge(G["w_ld"], 64 * h + 64)
                pe.wait_ge(G["z"], NCH * h + GATE_FREE)
                for c, (c0, n) in enumerate(CHUNKS):
                    mm(ps[:, c, 0:n], w_dec[:, :], rT[:, c0:c0 + n], start=True, stop=True).then_inc(G["gate"], 1)

            in_unit(0, 0, 2 * RANK)
            pe.wait_ge(in_moved, IN_FREE + NCH)
            pe.wait_ge(G["ones"], 1)
            pe.wait_ge(NM["mean"], NCH)
            with pe.Fori(0, GLA_HEADS) as i:
                in_unit(1, 3 * i + 1)
                gates(i)
                in_unit(2, 3 * i + 2)
                in_unit(0, 3 * i + 3)
            with pe.Fori(GLA_HEADS, IN_TILES // 3) as i:
                for j in range(3):
                    in_unit((1 + j) % 3, 3 * i + (j + 1))

            pe.wait_ge(in_moved, IN_FREE + NCH * (IN_TILES + 1))

            def turn(h, name, done, before, x):
                for c, (c0, n) in enumerate(CHUNKS):
                    if before:
                        pe.wait_ge(G[before], NCH * h + c + 1)
                    for t in range(c0 // P, (c0 + n) // P):
                        last = nc.tensor.transpose(ps[:, 4 + c, t * P - c0:(t + 1) * P - c0],
                                                   x[:, t * P:(t + 1) * P], ident[:, :])
                    last.then_inc(G[name], 1)

            def prepare(h):
                p = h % 2
                pe.wait_ge(G["ld_v"], 16 * (h + 1))
                if h:
                    pe.wait_ge(G["u_fw"], 4 * h)
                    pe.wait_ge(G["u_bw"], 4 * h)
                turn(h, "vT", "vN", None, gvT)
                pe.wait_ge(G["ks"], h + 1)
                turn(h, "kT", "kN", "vN", k_out[p])
                pe.wait_ge(G["qe"], h + 1)
                pe.wait_ge(G["ke"], h + 1)
                for c, (c0, n) in enumerate(CHUNKS):
                    if NCH * h + c:
                        pe.wait_ge(G["masked"], NCH * h + c)
                    for t in range(c0 // P, (c0 + n) // P):
                        for d in range(2):
                            rows = slice(d * DK, (d + 1) * DK)
                            last = mm(ps[:, d, t * P - c0:(t + 1) * P - c0], k_in[p][rows, t * P:(t + 1) * P],
                                      gq[p][rows, t * P:(t + 1) * P], start=True, stop=True)
                    last.then_inc(G["scores"], 1)

            prepare(0)
            for h in range(GLA_HEADS):
                p = h % 2
                pe.wait_ge(G["kN"], NCH * (h + 1))
                if h:
                    pe.wait_ge(G["o_kept"], NCH * h)
                for parity in range(2):
                    for n in range(parity, TOK // C, 2):
                        rows = slice(parity * C, parity * C + C)
                        last = mm(psf[:, u_col(n):u_col(n) + DV], gla_kn[rows, n // 2, :], gla_vn[p][rows, n // 2, :],
                                  start=True, stop=True)
                last.then_inc(G["u"], 1)
                if h + 1 < GLA_HEADS:
                    prepare(h + 1)
                pe.wait_ge(G["masked"], NCH * (h + 1))
                pe.wait_ge(G["state"], 2 * (h + 1))
                pe.wait_ge(G["u_fw"], 4 * (h + 1))
                for c, (c0, n) in enumerate(CHUNKS):
                    for t in range(c0 // P, (c0 + n) // P):
                        o = ps[:, O_BANKS[c], t * P - c0:(t + 1) * P - c0]
                        mm(o, gla_vn[p][:, t, :], gla_a[p][:, t, :], start=True, stop=False)
                        for e in range(2):
                            m = 2 * t + e
                            last = mm(o[:, e * C:(e + 1) * C], gla_s[p][:, :, m],
                                      gq[p][:, m * C:(m + 1) * C], start=False, stop=(e == 1))
                    last.then_inc(G["o"], 1)
            for h in range(GLA_HEADS):
                for c, (c0, n) in enumerate(CHUNKS):
                    pe.wait_ge(gn["square"], NCH * h + c + 1)
                    if h:
                        pe.wait_ge(gn["mean"], NCH * (h - 1) + c + 1)
                    mm(ps[:, c, 0:n], ones[:, :], gsq[c][:, 0:n], start=True, stop=True).then_inc(gn["sum"], 1)

            pe.wait_ge(T["ld"], 7 * 16)
            for c, (c0, n) in enumerate(CHUNKS):
                for t in range(c0 // P, (c0 + n) // P):
                    last = nc.tensor.transpose(ps[:, 4 + c, t * P - c0:(t + 1) * P - c0],
                                               vT[:, t * P:(t + 1) * P], ident[:, :])
                last.then_inc(T["vT"], 1)
            pe.wait_ge(const_bf, 1)
            pe.wait_ge(T["pads"], 4)
            pe.wait_ge(T["keys"], 1)
            pe.wait_ge(T["window"], 1)
            pe.wait_ge(T["vN"], 3)
            pe.wait_ge(gn["gated"], NCH * GLA_HEADS)

            def attend(u, i, r, first, drain):
                if not drain:
                    t, blk = r % 4, 2 * i + r // 4
                    pe.wait_ge(T["qrot"], blk + 1)
                    pe.wait_ge(T["p"], 2 * u + 2)
                    for e in range(2):
                        bank = 2 * (r % 2) + e
                        edges = ps[:, bank, 0:4 * P].rearrange("p (a s q) -> p a s q", a=2, s=2)[:, :, 0, :]
                        mm(edges, ident_bf[:, :], window[:, bass.ds(blk, 1), :, :].rearrange("p b s k -> p (b s) k"),
                           start=True, stop=False, skip_group_check=True)
                        last = mm(ps[:, bank, 0:3 * P], q_rot[r // 4][:, 2 * t + e, :],
                                  kT[:, 2 * t // HPG, bass.ds(blk * P, 3 * P)], start=False, stop=True, skip_group_check=True)
                    last.then_inc(T["s"], 1)
                if not (first and r < 3) and not (drain and r >= 3):
                    blk = 2 * i + (r - 3) // 4
                    pe.wait_ge(T["pT_act"], PT_FREE + u - 2)
                    pe.wait_ge(T["pT_dve"], PT_FREE + u - 2)
                    pe.wait_ge(T["o_nat"], 2 * u - 4)
                    g = 2 * ((r - 3) % 4) // HPG
                    for e in range(2):
                        for j in range(3):
                            last = mm(ps[:, 6, e * HD:(e + 1) * HD], probsT[:, e, j, :],
                                      vN[:, bass.ds(blk + j, 1), g * HD:(g + 1) * HD].rearrange("p a d -> p (a d)"),
                                      start=(j == 0), stop=(j == 2))
                    last.then_inc(T["pv"], 1)
                if not (first and r < 2) and not (drain and r >= 2):
                    pe.wait_ge(T["p"], P_FREE + 2 * u - 2)
                    pe.wait_ge(T["pT_act"], u - 1)
                    pe.wait_ge(T["pT_dve"], u - 1)
                    for e in range(2):
                        for j in range(3):
                            last = nc.tensor.transpose(ps[:, 4 + e, j * P:(j + 1) * P],
                                                       probs[(r - 2) % 4][:, e, j * P:(j + 1) * P], ident[:, :])
                    last.then_inc(T["turned"], 1)
                if not (first and r < 4):
                    pe.wait_ge(T["o_nat"], ON_FREE + 2 * u - 6)
                    pe.wait_ge(T["o_kept"], u - 3)
                    nc.tensor.transpose(ps[:, 7, 0:P], o_nat[(r - 4) % 2][:, :], ident[:, :]).then_inc(T["oT"], 1)

            for r in range(8):
                attend(r, 0, r, True, False)
            with pe.Fori(1, TT // 2) as i:
                for r in range(8):
                    attend(8 * i + r, i, r, False, False)
            for r in range(4):
                attend(TT // 2 * 8 + r, TT // 2, r, False, True)

            def out_unit(n, slot):
                pe.wait_ge(w_lo_ready, LO + U_OUT + n + 1)
                for c in range(NCH):
                    pe.wait_ge(o_lo, KT * (c + 1))
                    pe.wait_ge(out_added, NCH * n + c + 1)
                    project(c, c, slot).then_inc(out_done, 1)

            def tile_sums(k):
                for c, (_, n) in enumerate(CHUNKS):
                    pe.wait_ge(N2["square"], NCH * k + c + 1)
                    mm(ps[:, 4 + c, 0:n], ones[:, :], square[c][:, 0:n], start=(k == 0), stop=(k == KT - 1)
                       ).then_inc(N2["sum"], 1)

            for n in range(KT):
                out_unit(n, (U_OUT + n) % SPLIT)
                if n:
                    tile_sums(n - 1)
            tile_sums(KT - 1)
            ffn(A2, N2, U_FFN2, NF)
            for t in range(TT):
                pe.wait_ge(y_scaled, KT * (t + 1))
                if t >= 2:
                    pe.wait_ge(y_kept, 2 * t - 2)
                for half in range(2):
                    for k in range(4):
                        last = nc.tensor.transpose(ps[:, 4 + 2 * (t % 2) + half, k * P:(k + 1) * P],
                                                   normed[t % 2][:, 4 * half + k, :], ident[:, :])
                    last.then_inc(y_turned, 1)


def shape_constants():
    half = HD // 2
    inv_freq = np.float32(10000.0) ** (-np.arange(half, dtype=np.float32) / np.float32(half))
    pos = np.concatenate([np.arange(s, dtype=np.float32) for s in SEQS])
    ang = inv_freq[:, None] * pos[None, :]
    cos = np.concatenate([np.cos(ang), np.cos(ang)]).astype(np.float32)
    sin = np.concatenate([-np.sin(ang), np.sin(ang)]).astype(np.float32)
    window = np.zeros((P, TT, 2, P), np.float32)
    q, k = np.arange(P)[:, None], np.arange(P)[None, :]
    first = [0, SEQS[0] // P]
    last = [SEQS[0] // P - 1, TT - 1]
    for b in range(TT):
        window[:, b, 0] = np.where((k >= q) & (b not in first), 0.0, NEG)
        window[:, b, 1] = np.where((k <= q) & (b not in last), 0.0, NEG)
    j, i = np.arange(P)[:, None], np.arange(P)[None, :]
    same = j // C == i // C
    masks = np.stack([same & (i >= j), same & (i < j)]).astype(np.float32)
    reset = np.ones((P, TOK), np.float32)
    reset[:DK, 0::C] = 0.0
    reset[DK:, C - 1::C] = 0.0
    return {"c_ident": np.eye(P, dtype=np.float32), "c_cos": cos, "c_sin": sin, "c_window": window,
            "c_gla_masks": masks, "c_reset": reset}


_INS = ["x_prompt", "x_sample", "norm_ffn1", "w_ffn1_gate", "w_ffn1_up", "w_ffn1_down", "norm_mix", "w_in",
        "attn_sink", "w_gla_decay_fwd", "b_gla_decay_fwd", "w_gla_decay_bwd", "b_gla_decay_bwd", "gla_out_norm",
        "w_out", "norm_ffn2", "w_ffn2_gate", "w_ffn2_up", "w_ffn2_down", "norm_final"]


def kernel(**inputs):
    import concourse.bacc as bacc
    from concourse.bass_utils import run_bass_kernel_spmd

    nc = bacc.Bacc("TRN2", target_bir_lowering=False, num_devices=1)
    arrays, args = {}, []
    for name, a in [(n, inputs[n]) for n in _INS] + list(shape_constants().items()):
        a = np.ascontiguousarray(a)
        arrays[f"in_{name}"] = a
        args.append(nc.dram_tensor(f"in_{name}", a.shape, mybir.dt.from_np(a.dtype), kind="ExternalInput").ap())
    for n, s in enumerate(SEQS):
        args.append(nc.dram_tensor(f"out_{n}", (1, s, D_MODEL), F32, kind="ExternalOutput").ap())
    args.append(nc.dram_tensor("proj", (ROW_E + 3 * GLA_HEADS * P, TOK), F32, kind="Internal").ap())
    build(nc, *args)
    r = run_bass_kernel_spmd(nc, [arrays], core_ids=[0])
    return tuple(r.results[0][f"out_{n}"] for n in range(2))
```

```python
from contextlib import ExitStack

import concourse.bass as bass
import numpy as np
from concourse import mybir

F32 = mybir.dt.float32
F32R = mybir.dt.float32r
BF16 = mybir.dt.bfloat16
ALU = mybir.AluOpType
ACT = mybir.ActivationFunctionType
AX = mybir.AxisListType

P = 128
D_MODEL = 1024
KT = D_MODEL // P
SEQS = (256, 1024)
TOK = sum(SEQS)
TT = TOK // P
D_FF = 2816
GROUPS = D_FF // (2 * P)
CHUNKS = ((0, 512), (512, 512), (1024, 256))
NCH = len(CHUNKS)
EPS = 1e-6

HEADS, KV, HD = 8, 2, 64
HPG = HEADS // KV
GLA_HEADS, DK, DV, RANK = 4, 64, 128, 16
GATE_NORM = 16.0
C = 64
SEQ_CHUNKS = tuple(s // C for s in SEQS)
ROW_AK = HEADS * HD
ROW_AV = ROW_AK + KV * HD
ROW_GQ = ROW_AV + KV * HD
ROW_GK = ROW_GQ + GLA_HEADS * DK
ROW_GV = ROW_GK + GLA_HEADS * DK
ROW_GG = ROW_GV + GLA_HEADS * DV
ROW_R = ROW_GG + GLA_HEADS * DV
IN_W = ROW_R + 2 * RANK
IN_TILES = IN_W // P

ROW_E = IN_TILES * P

RAW, SPLIT = 3, 3
U_IN = 6 * GROUPS
U_OUT = U_IN + 1 + IN_TILES
U_FFN2 = U_OUT + KT
U_END = U_FFN2 + 6 * GROUPS
NEG = -1e30


def build(nc, x_prompt, x_sample, norm_ffn1, w_ffn1_gate, w_ffn1_up, w_ffn1_down, norm_mix, w_in, attn_sink,
          w_gla_decay_fwd, b_gla_decay_fwd, w_gla_decay_bwd, b_gla_decay_bwd, gla_out_norm, w_out, norm_ffn2,
          w_ffn2_gate, w_ffn2_up, w_ffn2_down, norm_final, c_ident, c_cos, c_sin, c_window, c_gla_masks, c_reset,
          y_prompt, y_sample, proj):
    ctx = ExitStack()
    with ctx:
        def sb(name, shape, dt=F32, scope=ctx):
            return scope.enter_context(nc.sbuf_tensor(name, shape, dt))

        def sem(name):
            return ctx.enter_context(nc.semaphore(name))

        xT = sb("xT", [P, KT, TOK])
        w_raw = [sb(f"w_raw{s}", [P, KT, P]) for s in range(RAW)]
        w_hi = [sb(f"w_hi{s}", [P, KT, P], F32R) for s in range(SPLIT)]
        w_lo = [sb(f"w_lo{s}", [P, KT, P], F32R) for s in range(SPLIT)]
        ident = sb("ident", [P, P])
        ident_bf = sb("ident_bf", [P, P], BF16)
        ones = sb("ones", [P, P])
        gains = sb("gains", [P, 4, KT])
        gla_gain = sb("gla_gain", [P, 1])
        sinks = sb("sinks", [P, HEADS])
        neg_sinks = sb("neg_sinks", [P, HEADS])

        with ExitStack() as s:
            hid_hi = sb("hid_hi", [P, 2, TOK], F32R, s)
            hid_lo = sb("hid_lo", [P, 2, TOK], F32R, s)
            scaled_g, scaled_u, silu, prod = ([sb(f"{n}{j}", [P, 512], scope=s) for j in range(2)]
                                              for n in ("scaled_g", "scaled_u", "silu", "prod"))
        with ExitStack() as s:
            stage = [sb(f"stage{j}", [P, TOK], scope=s) for j in range(3)]
        with ExitStack() as s:
            s.enter_context(nc.sbuf_tensor("under_stage", [P, 3, TOK], F32))
            rT = sb("rT", [2 * RANK + 1, TOK], scope=s)
            reset = sb("reset", [P, TOK], scope=s)
            gla_z = sb("gla_z", [P, TOK], scope=s)
            gla_t = sb("gla_t", [P, TOK], scope=s)
            gla_b = sb("gla_b", [P, TOK], scope=s)
        with ExitStack() as s:
            gla_s = [sb(f"gla_s{j}", [P, DV, TOK // C], scope=s) for j in range(2)]
        with ExitStack() as s:
            s.enter_context(nc.sbuf_tensor("under_o", [P, KT - 1, TOK], F32))
            masks = sb("masks", [P, 2, P], scope=s)
        with ExitStack() as s:
            gg = sb("gg", [P, GLA_HEADS, TOK], scope=s)
        with ExitStack() as s:
            x_in = [sb(f"x_in{t}", [P, D_MODEL], scope=s) for t in range(TT)]
        o_raw = sb("o_raw", [P, KT, TOK])
        with ExitStack() as s:
            h_hi = sb("h_hi", [P, KT, TOK], F32R, s)
            h_lo = sb("h_lo", [P, KT, TOK], F32R, s)
            rstd = sb("rstd", [P, TOK], scope=s)
            with ExitStack() as r:
                square = [sb(f"square{j}", [P, CHUNKS[j][1]], scope=r) for j in range(NCH)]
            w_dec = sb("w_dec", [2 * RANK + 1, P], scope=s)
        with ExitStack() as s:
            normed = sb("normed", [P, KT, TOK], scope=s)
            y_out = [sb(f"y_out{j}", [P, D_MODEL], scope=s) for j in range(4)]
        with ExitStack() as s:
            gq = [sb(f"gq{j}", [P, TOK], scope=s) for j in range(3)]
            e_fw = [sb(f"e_fw{j}", [P, TOK], scope=s) for j in range(2)]
            k_in = [sb(f"k_in{j}", [P, TOK], scope=s) for j in range(2)]
            k_out = [sb(f"k_out{j}", [P, TOK], scope=s) for j in range(2)]
            gk = sb("gk", [P, TOK], scope=s)
            gvT = sb("gvT", [P, TOK], scope=s)
            gla_vn = [sb(f"gla_vn{j}", [P, TT, DV], scope=s) for j in range(2)]
            gla_kn = sb("gla_kn", [P, TT, P], scope=s)
            gla_a = [sb(f"gla_a{j}", [P, TT, P], scope=s) for j in range(2)]
            gla_dec = sb("gla_dec", [P, DV, TOK // C], scope=s)
        with ExitStack() as s:
            gsq_last = sb("gsq_last", [P, TOK], scope=s)
        with ExitStack() as s:
            q_in1, q_sw1, probsT = sb("q_in1", [HD, HEADS, P], scope=s), sb("q_sw1", [HD, HEADS, P], scope=s), \
                sb("probsT", [P, 2, 3, P], scope=s)
            grs = sb("grs", [P, GLA_HEADS * TT], scope=s)
            q_in = [sb("q_in0", [HD, HEADS, P], scope=s), q_in1]
            q_sw = [sb("q_sw0", [HD, HEADS, P], scope=s), q_sw1]
            q_rot = [sb(f"q_rot{j}", [HD, HEADS, P], scope=s) for j in range(2)]
            kT = sb("kT", [HD, KV, TOK + 2 * P], scope=s)
            vN = sb("vN", [P, TT + 2, P], scope=s)
            window = sb("window", [P, TT, 2, P], BF16, s)
            cos = sb("cos", [HD, TOK], scope=s)
            sin = sb("sin", [HD, TOK], scope=s)
            o_nat = [sb(f"o_nat{j}", [P, P], scope=s) for j in range(2)]
            stats = [sb(f"stats{j}", [P, 6, 2], scope=s) for j in range(4)]
            with ExitStack() as r:
                probs = [sb(f"probs{j}", [P, 2, 3 * P], scope=r) for j in range(4)]
            with ExitStack() as r:
                vT = sb("vT", [P, TOK], scope=r)
                k_sw = sb("k_sw", [HD, KV, TOK], scope=r)
                window_f = sb("window_f", [P, TT, 2, P], scope=r)
        MX, NEGM, DSINK, SUM, ESINK, RDEN = range(6)

        ps = ctx.enter_context(nc.psum_tensor("ps", [P, 8, 512], F32))
        GU, DN = 0, 4
        O_BANKS = (2, 3, 7)
        SUMS = (2, 3, 2)
        psf = ps[:, :, :].rearrange("p b n -> p (b n)")

        ld_const, const_bf, const_ones, const_neg = (sem(n) for n in ("ld_const", "const_bf", "const_ones", "const_neg"))
        w_loaded = [sem(f"w_loaded{s}") for s in range(RAW)]
        w_hi_ready, w_lo_ready = sem("w_hi_ready"), sem("w_lo_ready")
        LO = RAW
        x_loaded = [sem(f"x_loaded{c}") for c in range(NCH)]
        x_turned, x_kept_act, x_kept_dve = sem("x_turned"), sem("x_kept_act"), sem("x_kept_dve")

        def named(prefix, names):
            return {k: sem(f"{prefix}_{k}") for k in names.split()}

        norm_names = "square sum mean sqrt rstd"
        N1, NM, N2 = (named(n, norm_names + " hi lo") for n in ("norm_ffn1", "norm_mix", "norm_ffn2"))
        NF = named("norm_final", norm_names)
        ffn_names = "gate_used gu_done gate_rs up_rs silu prod hid_hi hid_lo dn_done dn_added"
        A1, A2 = named("ffn1", ffn_names), named("ffn2", ffn_names)
        GU_FREE, DN_USED, DN_FREE = 2, 1, 4
        in_done, in_moved = sem("in_done"), sem("in_moved")
        IN_USED, IN_FREE = 2 * NCH, NCH
        GATE_FREE = NCH
        in_stored = [sem(f"in_stored{j}") for j in range(3)]
        o_hi, o_lo, out_done, out_added = (sem(n) for n in ("o_hi", "o_lo", "out_done", "out_added"))
        G = named("gla", "zeroed ones w_ld ld_tables gate z abs exp ln log scan eb enb diff es e_stored ld_k ld_v "
                         "qe ks ke decay s_zeroed vT vN kT kN scores masking masked u u_fw u_bw state o o_kept")
        e_ld = [sem(f"gla_ld{j}") for j in range(2)]
        q_ld = [sem(f"gla_q_ld{j}") for j in range(3)]
        gn = named("gla_norm", "ld silu square sum mean sqrt rstd spread scaled gated")
        T = named("attn", "ld pads cosd sind keys vT vN window qcos qsin qrot s max negm dsink p es den rden turned "
                          "pT_act pT_dve pv o_nat oT o_kept")
        S_FREE, P_FREE, PT_FREE, ON_FREE, OT_FREE = 8, 4, 1, 2, 1
        t_ld = [sem(f"attn_ld{j}") for j in range(2)]
        y_scaled, y_turned, y_kept = sem("y_scaled"), sem("y_turned"), sem("y_kept")
        y_stored = [sem(f"y_stored{j}") for j in range(4)]
        N_CONST_LD = 7

        def col_unit(w, col, cols=P):
            return w[0].rearrange("(k p) n -> p k n", p=P)[:, :, bass.ds(col, cols)]

        def row_unit(w, row):
            return w[0][bass.ds(row, P), :].rearrange("p (k n) -> p k n", k=KT)

        gsq = [o_raw[:, 6, :], o_raw[:, 6, :], o_raw[:, 7, :], gsq_last[:, :]]
        GLA_SUMS = 7 * 512 + 2 * P

        def u_col(n):
            return (2 + 3 * (n % 2)) * 512 + n // 2 * DV

        first_chunks = (0, SEQ_CHUNKS[0])
        last_chunks = (SEQ_CHUNKS[0] - 1, TOK // C - 1)

        block = ctx.enter_context(nc.Block())

        @block.sync
        def _(sp):
            sp.dma_start(ident[:, :], c_ident).then_inc(ld_const, 16)

            def x_load(t):
                src = x_prompt[0][t * P:(t + 1) * P, :] if t < 2 else x_sample[0][(t - 2) * P:(t - 1) * P, :]
                sp.dma_start(x_in[t][:, :], src).then_inc(x_loaded[t // 4], 16)

            for t in range(4):
                x_load(t)
            with nc.allow_non_contiguous_dma(reason="small parameter columns"):
                for n, g in enumerate((norm_ffn1[0], norm_mix[0], norm_ffn2[0], norm_final)):
                    sp.dma_start(gains[:, n, :], g.rearrange("(k p) -> p k", p=P)).then_inc(ld_const, 16)
                sp.dma_start(gla_gain[:, :], gla_out_norm.rearrange("a p -> p a")).then_inc(ld_const, 16)
            sp.dma_start(sinks[:, :], attn_sink[0:1, :].to_broadcast([P, HEADS])).then_inc(ld_const, 16)

            def load_unit(unit, slot, src, cols=P):
                sp.wait_ge(w_lo_ready, unit + 1)
                sp.dma_start(w_raw[slot][:, :, 0:cols], src).then_inc(w_loaded[slot], 16)

            def ffn_units(base, wg, wu, wd, i):
                for j, src in enumerate((col_unit(wg, i * 2 * P), col_unit(wu, i * 2 * P),
                                         col_unit(wg, i * 2 * P + P), col_unit(wu, i * 2 * P + P),
                                         row_unit(wd, i * 2 * P), row_unit(wd, i * 2 * P + P))):
                    load_unit(base + j + 6 * i, j % RAW, src)

            for j, w in enumerate((w_ffn1_gate, w_ffn1_up)):
                load_unit(j, j, col_unit(w, 0))
            for t in range(4, TT):
                x_load(t)
            for j, src in enumerate((col_unit(w_ffn1_gate, P), col_unit(w_ffn1_up, P),
                                     row_unit(w_ffn1_down, 0), row_unit(w_ffn1_down, P)), 2):
                load_unit(j, j % RAW, src)
            with sp.Fori(1, GROUPS) as i:
                ffn_units(0, w_ffn1_gate, w_ffn1_up, w_ffn1_down, i)
            load_unit(U_IN, 0, col_unit(w_in, ROW_R, 2 * RANK), 2 * RANK)
            with sp.Fori(0, IN_TILES // 3) as i:
                for j in range(3):
                    load_unit(U_IN + 1 + 3 * i + j, (1 + j) % RAW, col_unit(w_in, i * 3 * P + j * P))
            for u in range(U_OUT, U_OUT + RAW):
                load_unit(u, u % RAW, col_unit(w_out, (u - U_OUT) * P))

            for j in range(3):
                sp.wait_ge(in_stored[j], 16 + 16 * IN_TILES // 3)
            sp.wait_ge(G["e_stored"], 48 * (GLA_HEADS + 1))
            sp.wait_ge(in_done, IN_USED + NCH * (IN_TILES + 1))

            def load_q(h):
                for half in range(2):
                    sp.dma_start(gq[h % 3][half * DK:(half + 1) * DK, :],
                                 proj[h * DK + ROW_GQ:(h + 1) * DK + ROW_GQ, :]).then_inc(q_ld[h % 3], 16)

            def load_decays(h):
                for e, to in enumerate((e_fw, k_in, k_out)):
                    row = ROW_E + (3 * h + e) * P
                    sp.dma_start(to[h % 2][:, :], proj[row:row + P, :]).then_inc(e_ld[h % 2], 16)

            def load_k(h):
                for half in range(2):
                    sp.dma_start(gk[half * DK:(half + 1) * DK, :], proj[h * DK + ROW_GK:(h + 1) * DK + ROW_GK, :]
                                 ).then_inc(G["ld_k"], 16)

            def load_v(h):
                sp.dma_start(gvT[:, :], proj[h * DV + ROW_GV:(h + 1) * DV + ROW_GV, :]).then_inc(G["ld_v"], 16)

            load_k(0)
            load_decays(0)
            load_q(0)
            load_v(0)
            sp.dma_start(masks[:, :, :], c_gla_masks.rearrange("m p n -> p m n")).then_inc(G["ld_tables"], 16)
            load_decays(1)
            load_q(1)
            load_q(2)
            for h in range(1, GLA_HEADS):
                sp.wait_ge(G["vT"], NCH * h)
                load_v(h)
                sp.wait_ge(G["ks"], h)
                sp.wait_ge(G["ke"], h)
                load_k(h)
                if h + 1 < GLA_HEADS:
                    sp.wait_ge(G["kT"], NCH * h)
                    sp.wait_ge(G["scores"], NCH * h)
                    sp.wait_ge(G["qe"], h)
                    sp.wait_ge(G["decay"], 4 * h)
                    load_decays(h + 1)
                if h + 2 < GLA_HEADS:
                    sp.wait_ge(G["o"], NCH * h)
                    load_q(h + 2)
            ak = proj[ROW_AK:ROW_AK + KV * HD, :].rearrange("(g d) n -> d g n", d=HD)
            aq = proj[0:HEADS * HD, :].rearrange("(h d) n -> d h n", d=HD)
            halves = [(slice(a * HD // 2, (a + 1) * HD // 2), slice((1 - a) * HD // 2, (2 - a) * HD // 2)) for a in range(2)]

            def load_gate(h):
                sp.dma_start(gg[:, h, :], proj[ROW_GG + h * DV:ROW_GG + (h + 1) * DV, :]).then_inc(gn["ld"], 16)

            def q_loads(b, p):
                cols = bass.ds(b * P, P)
                sp.dma_start(q_in[p][:, :, :], aq[:, :, cols]).then_inc(t_ld[p], 16)
                for to, of in halves:
                    sp.dma_start(q_sw[p][to, :, :], aq[of, :, cols]).then_inc(t_ld[p], 16)

            sp.wait_ge(G["o"], NCH * (GLA_HEADS - 1))
            sp.wait_ge(G["scores"], NCH * GLA_HEADS)
            sp.wait_ge(G["kT"], NCH * GLA_HEADS)
            load_gate(0)
            load_gate(1)
            sp.dma_start(kT[:, :, P:P + TOK], ak).then_inc(T["ld"], 16)
            sp.dma_start(cos[:, :], c_cos).then_inc(T["ld"], 16)
            sp.wait_ge(G["o"], NCH * GLA_HEADS)
            load_gate(2)
            load_gate(3)
            for to, of in halves:
                sp.dma_start(k_sw[to, :, :], ak[of, :, :]).then_inc(T["ld"], 16)
            sp.dma_start(sin[:, :], c_sin).then_inc(T["ld"], 16)
            sp.dma_start(vT[:, :], proj[ROW_AV:ROW_AV + KV * HD, :]).then_inc(T["ld"], 16)
            q_loads(0, 0)
            sp.dma_start(window_f[:, :, :, :], c_window).then_inc(T["ld"], 16)
            sp.wait_ge(gn["sum"], GLA_HEADS)
            q_loads(1, 1)
            with sp.Fori(1, TT // 2) as i:
                for p in range(2):
                    sp.wait_ge(T["qrot"], 2 * i + p - 1)
                    q_loads(2 * i + p, p)

            for u in range(U_OUT + RAW, U_FFN2):
                load_unit(u, u % RAW, col_unit(w_out, (u - U_OUT) * P))
            with sp.Fori(0, GROUPS) as i:
                ffn_units(U_FFN2, w_ffn2_gate, w_ffn2_up, w_ffn2_down, i)

            for t in range(TT):
                sp.wait_ge(y_kept, 2 * t + 2)
                dst = y_prompt[0][t * P:(t + 1) * P, :] if t < 2 else y_sample[0][(t - 2) * P:(t - 1) * P, :]
                sp.dma_start(dst, y_out[t % 4][:, :]).then_inc(y_stored[t % 4], 16)
            for j in range(4):
                sp.wait_ge(y_stored[j], 16 * len(range(j, TT, 4)))

        @block.gpsimd
        def _(pool):
            pool.sem_inc(w_lo_ready, LO)

            def split_lo(unit, slot):
                pool.wait_ge(w_hi_ready, unit + 1)
                nc.gpsimd.tensor_tensor(w_lo[slot][:, :, :], w_raw[slot][:, :, :], w_hi[slot][:, :, :].bitcast(F32),
                                        ALU.subtract).then_inc(w_lo_ready, 1)

            early = U_OUT + RAW
            with pool.Fori(0, early // 3) as i:
                for j in range(3):
                    split_lo(3 * i + j, j)
            for u in range(early // 3 * 3, early):
                split_lo(u, u % 3)

            for h in range(GLA_HEADS):
                p = h % 2
                pool.wait_ge(e_ld[p], 48 * (h // 2 + 1))
                pool.wait_ge(G["ld_k"], 32 * (h + 1))
                nc.gpsimd.tensor_tensor(k_in[p][:, :], gk[:, :], k_in[p][:, :], ALU.mult).then_inc(G["ke"], 1)
                nc.gpsimd.tensor_tensor(k_out[p][:, :], gk[:, :], k_out[p][:, :], ALU.mult).then_inc(G["ks"], 1)
            pool.wait_ge(G["o_kept"], NCH * GLA_HEADS)
            pool.wait_ge(gn["square"], GLA_HEADS)
            for h in range(GLA_HEADS):
                pool.wait_ge(gn["silu"], h + 1)
                nc.gpsimd.tensor_tensor(o_raw[:, 4 + h, :], o_raw[:, 4 + h, :], gg[:, h, :], ALU.mult
                                        ).then_inc(gn["gated"], 1)

            pool.wait_ge(T["ld"], 7 * 16)
            with pool.Fori(0, TT // 2) as i:
                for p in range(2):
                    b = 2 * i + p
                    cols = bass.ds(b * P, P)
                    pool.wait_ge(t_ld[p], 48 * i + 48)
                    nc.gpsimd.tensor_tensor(q_in[p][:, :, :], q_in[p][:, :, :],
                                            cos[:, cols].unsqueeze(1).to_broadcast([HD, HEADS, P]),
                                            ALU.mult).then_inc(T["qcos"], 1)
                    nc.gpsimd.tensor_tensor(q_sw[p][:, :, :], q_sw[p][:, :, :],
                                            sin[:, cols].unsqueeze(1).to_broadcast([HD, HEADS, P]),
                                            ALU.mult).then_inc(T["qsin"], 1)
                    pool.wait_ge(T["qcos"], b + 1)
                    pool.wait_ge(T["qsin"], b + 1)
                    pool.wait_ge(T["s"], HPG * b - 2 * HPG + S_FREE + 4)
                    nc.gpsimd.tensor_tensor(q_rot[p][:, :, :], q_in[p][:, :, :], q_sw[p][:, :, :],
                                            ALU.add).then_inc(T["qrot"], 1)

            rest = U_END - early
            with pool.Fori(0, rest // 3) as i:
                for j in range(3):
                    split_lo(early + 3 * i + j, (early + j) % 3)
            for u in range(early + rest // 3 * 3, U_END):
                split_lo(u, u % 3)

        @block.scalar
        def _(act):
            for j in range(3):
                act.sem_inc(in_stored[j], 16)
            act.sem_inc(G["e_stored"], 48)
            act.sem_inc(G["z"], GATE_FREE)
            act.sem_inc(T["p"], P_FREE)
            act.sem_inc(T["pT_act"], PT_FREE)
            act.sem_inc(T["o_kept"], OT_FREE)

            def split_hi(unit, slot):
                act.wait_ge(w_loaded[slot], 16 * (unit // RAW + 1))
                nc.scalar.activation(w_hi[slot][:, :, :], w_raw[slot][:, :, :], ACT.Copy).then_inc(w_hi_ready, 1)

            def loads_of(base, per, i, j):
                return 16 * (base // RAW + j // RAW + 1) + 16 * (per // RAW) * i

            def gained_hi(N, gain, c, k):
                c0, n = CHUNKS[c]
                nc.scalar.activation(h_hi[:, k, c0:c0 + n], xT[:, k, c0:c0 + n], ACT.Copy,
                                     scale=gains[:, gain, k:k + 1]).then_inc(N["hi"], 1)

            def squares(N, c, k, idx, ring):
                c0, n = CHUNKS[c]
                if idx >= ring:
                    act.wait_ge(N["sum"], idx - ring + 1)
                nc.scalar.activation(square[idx % ring][:, 0:n], xT[:, k, c0:c0 + n], ACT.Square
                                     ).then_inc(N["square"], 1)

            def root(N, c):
                c0, n = CHUNKS[c]
                act.wait_ge(N["mean"], c + 1)
                nc.scalar.activation(rstd[:, c0:c0 + n], rstd[:, c0:c0 + n], ACT.Sqrt).then_inc(N["sqrt"], 1)

            def ffn_body(A, base, i, first=False, last=False):
                def split(j):
                    act.wait_ge(w_loaded[j % RAW], loads_of(base, 6, i, j))
                    nc.scalar.activation(w_hi[j % SPLIT][:, :, :], w_raw[j % RAW][:, :, :],
                                         ACT.Copy).then_inc(w_hi_ready, 1)

                act.wait_ge(A["dn_done"], DN_USED + 24 * i)
                if not first:
                    split(1)
                split(2)
                for s in range(6):
                    t, (c0, n) = s // NCH, CHUNKS[s % NCH]
                    if s % NCH == 2:
                        act.wait_ge(A["gate_used"], 2 * i + t + 1)
                        split(3 + 2 * t)
                    act.wait_ge(A["gate_rs"], 6 * i + s + 1)
                    nc.scalar.activation(silu[s % 2][:, 0:n], scaled_g[s % 2][:, 0:n], ACT.Silu).then_inc(A["silu"], 1)
                    act.wait_ge(A["prod"], 6 * i + s + 1)
                    nc.scalar.activation(hid_hi[:, t, c0:c0 + n], prod[s % 2][:, 0:n],
                                         ACT.Copy).then_inc(A["hid_hi"], 1)
                    if s % NCH == 2 and not (last and t == 1):
                        act.wait_ge(A["gu_done"], 6 * i + s + 1)
                        split(4 + 2 * t)

            for c, (c0, n) in enumerate(CHUNKS):
                for t in range(c0 // P, (c0 + n) // P):
                    act.wait_ge(x_turned, 2 * t + 1)
                    nc.scalar.copy(xT[:, 0:4, t * P:(t + 1) * P],
                                   ps[:, 4 + 2 * (t % 2), :].rearrange("p (k n) -> p k n", k=4)).then_inc(x_kept_act, 1)
                act.wait_ge(x_kept_act, (c0 + n) // P)
                act.wait_ge(x_kept_dve, (c0 + n) // P)
                if c == 0:
                    act.wait_ge(ld_const, 16 * N_CONST_LD)
                for k in range(KT):
                    gained_hi(N1, 0, c, k)
                if c == 0:
                    act.wait_ge(w_loaded[0], 16)
                    nc.scalar.activation(w_hi[0][:, :, :], w_raw[0][:, :, :], ACT.Copy).then_inc(w_hi_ready, 1)
                else:
                    for k in range(KT):
                        squares(N1, c - 1, k, KT * (c - 1) + k, 2)
                if c == 1:
                    split_hi(1, 1)
            for k in range(KT):
                squares(N1, NCH - 1, k, KT * (NCH - 1) + k, 2)
            for c in range(NCH):
                root(N1, c)
            ffn_body(A1, 0, 0, first=True)
            with act.Fori(1, GROUPS) as i:
                ffn_body(A1, 0, i)
            for c in range(NCH):
                for k in range(KT):
                    act.wait_ge(A1["dn_added"], DN_FREE + 24 * (GROUPS - 1) + KT * c + k + 1)
                    gained_hi(NM, 1, c, k)
                if c:
                    for k in range(KT):
                        squares(NM, c - 1, k, KT * (c - 1) + k, 2)
            root(NM, 0)
            root(NM, 1)
            for k in range(KT):
                squares(NM, NCH - 1, k, KT * (NCH - 1) + k, 2)
            split_hi(U_IN + 1, 1)
            root(NM, 2)

            act.dma_start(reset[:, :], c_reset).then_inc(G["ld_tables"], 16)
            act.wait_ge(G["zeroed"], 1)

            def split_ahead(i, j, w):
                act.wait_ge(in_done, IN_USED + NCH * w - NCH)
                act.wait_ge(w_loaded[(j + 1) % RAW], loads_of(U_IN, 3, i, j + 1))
                nc.scalar.activation(w_hi[(j + 1) % SPLIT][:, :, :], w_raw[(j + 1) % RAW][:, :, :],
                                     ACT.Copy).then_inc(w_hi_ready, 1)

            def store(j, w):
                act.wait_ge(in_moved, IN_FREE + NCH * w + NCH)
                act.dma_start(proj[bass.ds((w - 1) * P, P), :], stage[j][:, :]).then_inc(in_stored[j], 16)

            def load_decay(h):
                act.wait_ge(G["gate"], NCH * h + NCH)
                for half, (wd, bd) in enumerate(((w_gla_decay_fwd, b_gla_decay_fwd), (w_gla_decay_bwd, b_gla_decay_bwd))):
                    act.dma_start(w_dec[2 * RANK:2 * RANK + 1, half * DK:(half + 1) * DK],
                                  bd[:, bass.ds(h * DK, DK)]).then_inc(G["w_ld"], 16)
                    act.dma_start(w_dec[half * RANK:(half + 1) * RANK, half * DK:(half + 1) * DK],
                                  wd[0][:, bass.ds(h * DK, DK)]).then_inc(G["w_ld"], 16)

            def log_gate(h):
                act.wait_ge(G["e_stored"], 48 * h + 48)
                for c, (c0, n) in enumerate(CHUNKS):
                    act.wait_ge(G["gate"], NCH * h + NCH + c + 1)
                    nc.scalar.activation(gla_z[:, c0:c0 + n], ps[:, c, 0:n], ACT.Copy).then_inc(G["z"], 1)
                act.wait_ge(G["z"], GATE_FREE + NCH * h + NCH)
                nc.scalar.activation(gla_t[:, :], gla_z[:, :], ACT.Abs).then_inc(G["abs"], 1)
                act.wait_ge(G["abs"], h + 1)
                nc.scalar.activation(gla_t[:, :], gla_t[:, :], ACT.Exp, scale=-1.0).then_inc(G["exp"], 1)
                act.wait_ge(G["exp"], h + 1)
                nc.scalar.activation(gla_t[:, :], gla_t[:, :], ACT.Ln, bias=1.0).then_inc(G["ln"], 1)

            def decays(h):
                act.wait_ge(G["scan"], 2 * h + 2)
                nc.scalar.activation(gla_t[:, :], gla_b[:, :], ACT.Exp, scale=1.0 / GATE_NORM).then_inc(G["eb"], 1)
                act.wait_ge(G["diff"], 2 * h + 2)
                nc.scalar.activation(gla_z[:, :], gla_z[:, :], ACT.Exp, scale=1.0 / GATE_NORM).then_inc(G["es"], 1)
                act.wait_ge(G["eb"], h + 1)
                nc.scalar.activation(gla_b[:, :], gla_b[:, :], ACT.Exp, scale=-1.0 / GATE_NORM).then_inc(G["enb"], 1)
                act.wait_ge(G["enb"], h + 1)
                act.wait_ge(G["es"], h + 1)
                for e, decay in enumerate((gla_t, gla_b, gla_z)):
                    act.dma_start(proj[bass.ds(h * 3 * P + (ROW_E + e * P), P), :], decay[:, :]
                                  ).then_inc(G["e_stored"], 16)

            with act.Fori(0, GLA_HEADS) as i:
                load_decay(i)
                split_ahead(i, 1, 3 * i + 1)
                store(0, 3 * i + 1)
                split_ahead(i, 2, 3 * i + 2)
                log_gate(i)
                store(1, 3 * i + 2)
                split_ahead(i, 3, 3 * i + 3)
                decays(i)
                store(2, 3 * i + 3)
            with act.Fori(GLA_HEADS, IN_TILES // 3) as i:
                for j in range(3):
                    split_ahead(i, j + 1, 3 * i + (j + 1))
                    store(j, 3 * i + (j + 1))
            act.wait_ge(in_done, IN_USED + NCH * IN_TILES)
            split_hi(U_OUT + 1, (U_OUT + 1) % SPLIT)
            act.wait_ge(in_done, IN_USED + NCH * (IN_TILES + 1))
            split_hi(U_OUT + 2, (U_OUT + 2) % SPLIT)

            def turned(h, name, done, to):
                for c, (c0, n) in enumerate(CHUNKS):
                    act.wait_ge(G[name], NCH * h + c + 1)
                    nc.scalar.copy(to[:, c0 // P:(c0 + n) // P, :],
                                   ps[:, 4 + c, 0:n].rearrange("p (t d) -> p t d", d=P)).then_inc(G[done], 1)

            def spread(h):
                p = h % 2
                act.wait_ge(e_ld[p], 48 * (h // 2 + 1))
                if h:
                    act.wait_ge(G["state"], 2 * h)
                for a, b in zip(first_chunks, last_chunks):
                    n = b - a
                    nc.scalar.copy(gla_dec[DK:P, :, a:b],
                                   e_fw[p][DK:P, (a + 1) * C:b * C + 1:C].unsqueeze(1).to_broadcast([DK, DV, n])
                                   ).then_inc(G["decay"], 1)
                    nc.scalar.copy(gla_dec[0:DK, :, a + 1:b + 1],
                                   e_fw[p][0:DK, a * C + C - 1:b * C:C].unsqueeze(1).to_broadcast([DK, DV, n])
                                   ).then_inc(G["decay"], 1)

            turned(0, "vT", "vN", gla_vn[0])
            turned(0, "kT", "kN", gla_kn)
            act.wait_ge(G["s_zeroed"], 9)
            spread(0)
            for h in range(GLA_HEADS):
                if h >= 2:
                    act.wait_ge(G["o"], NCH * (h - 1))
                act.wait_ge(G["u"], h + 1)
                for start, parity in ((0, 0), (1, 1)):
                    for a, b in zip(first_chunks, last_chunks):
                        n = len(range(a + start, b, 2))
                        col = u_col(a + start)
                        nc.scalar.copy(gla_s[h % 2][0:DK, :, a + start + 1:b + 1:2],
                                       psf[0:DK, col:col + n * DV].rearrange("p (n d) -> p d n", d=DV)
                                       ).then_inc(G["u_fw"], 1)
                if h + 1 < GLA_HEADS:
                    turned(h + 1, "vT", "vN", gla_vn[(h + 1) % 2])
                    turned(h + 1, "kT", "kN", gla_kn)
                    spread(h + 1)
                for c, (c0, n) in enumerate(CHUNKS):
                    act.wait_ge(G["o"], NCH * h + c + 1)
                    nc.scalar.copy(o_raw[:, 4 + h, c0:c0 + n], ps[:, O_BANKS[c], 0:n]).then_inc(G["o_kept"], 1)
                if h:
                    act.wait_ge(gn["sum"], h)
                act.wait_ge(G["o_kept"], NCH * (h + 1))
                if h == 2:
                    act.wait_ge(G["masked"], NCH * GLA_HEADS)
                nc.scalar.activation(gsq[h], o_raw[:, 4 + h, :], ACT.Square).then_inc(gn["square"], 1)
            act.wait_ge(gn["ld"], 16 * GLA_HEADS)
            for h in range(GLA_HEADS):
                nc.scalar.activation(gg[:, h, :], gg[:, h, :], ACT.Silu).then_inc(gn["silu"], 1)
            act.wait_ge(gn["mean"], 1)
            nc.scalar.activation(grs[:, :], grs[:, :], ACT.Sqrt).then_inc(gn["sqrt"], 1)
            for j in range(3):
                act.wait_ge(T["vT"], j + 1)
                c0, n = CHUNKS[j]
                nc.scalar.copy(vN[:, 1 + c0 // P:1 + (c0 + n) // P, :],
                               ps[:, 4 + j, 0:n].rearrange("p (t d) -> p t d", d=P)).then_inc(T["vN"], 1)

            act.wait_ge(T["ld"], 7 * 16)
            nc.scalar.copy(window[:, :, :, :], window_f[:, :, :, :]).then_inc(T["window"], 1)
            act.wait_ge(T["window"], 1)
            act.wait_ge(T["keys"], 1)
            act.wait_ge(T["vN"], 3)

            def attend(u, i, r, first, drain):
                st = stats[r % 4]
                if not drain:
                    act.wait_ge(T["negm"], u + 1)
                    for e in range(2):
                        nc.scalar.activation(probs[r % 4][:, e, :], ps[:, 2 * (r % 2) + e, 0:3 * P], ACT.Exp,
                                             bias=st[:, NEGM, e:e + 1], scale=HD ** -0.5,
                                             accum_out=st[:, SUM, e:e + 1]).then_inc(T["p"], 1)
                    act.wait_ge(T["dsink"], u + 1)
                    nc.scalar.activation(st[:, ESINK, :], st[:, DSINK, :], ACT.Exp).then_inc(T["es"], 1)
                if not (first and r < 2) and not (drain and r >= 2):
                    act.wait_ge(T["turned"], u - 1)
                    nc.scalar.copy(probsT[:, 0, :, :],
                                   ps[:, 4, 0:3 * P].rearrange("p (j q) -> p j q", j=3)).then_inc(T["pT_act"], 1)
                if not (first and r < 4):
                    act.wait_ge(T["oT"], u - 3)
                    cols = bass.ds((2 * i + (r - 4) // 4) * P, P)
                    nc.scalar.copy(o_raw[:, (r - 4) % 4, cols], ps[:, 7, 0:P]).then_inc(T["o_kept"], 1)

            for r in range(8):
                attend(r, 0, r, True, False)
            with act.Fori(1, TT // 2) as i:
                for r in range(8):
                    attend(8 * i + r, i, r, False, False)
            for r in range(4):
                attend(TT // 2 * 8 + r, TT // 2, r, False, True)

            act.wait_ge(T["o_kept"], OT_FREE + HPG * TT)
            act.wait_ge(T["s"], S_FREE + HPG * TT)
            for c, (c0, n) in enumerate(CHUNKS):
                for k in range(KT):
                    nc.scalar.activation(h_hi[:, k, c0:c0 + n], o_raw[:, k, c0:c0 + n], ACT.Copy).then_inc(o_hi, 1)
            for n in range(KT):
                if n < KT - 2:
                    act.wait_ge(out_done, NCH * (n + 1))
                    split_hi(U_OUT + RAW + n, (U_OUT + RAW + n) % SPLIT)
                if n == KT - 1:
                    act.wait_ge(out_done, NCH * (KT - 1))
                    split_hi(U_FFN2 + 1, 1)
                for c in range(NCH):
                    act.wait_ge(out_added, IN_FREE + NCH * n + c + 1)
                    squares(N2, c, n, NCH * n + c, 3)
                    if n == KT - 1:
                        for k in (range(KT), range(6), range(0))[c]:
                            gained_hi(N2, 2, c, k)
            for c, k in ((1, 6), (1, 7), *((2, k) for k in range(KT))):
                gained_hi(N2, 2, c, k)
            for c in range(NCH):
                root(N2, c)
            ffn_body(A2, U_FFN2, 0, first=True)
            with act.Fori(1, GROUPS - 1) as i:
                ffn_body(A2, U_FFN2, i)
            ffn_body(A2, U_FFN2, GROUPS - 1, last=True)
            for c in range(NCH):
                for k in range(KT):
                    act.wait_ge(A2["dn_added"], DN_FREE + 24 * (GROUPS - 1) + KT * c + k + 1)
                    squares(NF, c, k, KT * c + k, 2)
                if c != 1:
                    root(NF, c // 2)
            root(NF, 2)
            for t in range(TT):
                for half in range(2):
                    act.wait_ge(y_turned, 2 * t + half + 1)
                    if t >= 4 and half == 0:
                        act.wait_ge(y_stored[t % 4], 16 * (t // 4))
                    nc.scalar.copy(y_out[t % 4][:, half * 512:(half + 1) * 512],
                                   ps[:, 4 + 2 * (t % 2) + half, :]).then_inc(y_kept, 1)

        @block.vector
        def _(dve):
            v = nc.vector
            for A in (A1, A2):
                dve.sem_inc(A["up_rs"], GU_FREE)
                dve.sem_inc(A["dn_added"], DN_FREE)
            dve.sem_inc(in_moved, IN_FREE)
            dve.sem_inc(out_added, IN_FREE)
            dve.sem_inc(T["pT_dve"], PT_FREE)
            dve.sem_inc(T["o_nat"], ON_FREE)
            v.memset(ones[:, :], 1.0).then_inc(const_ones, 1)
            dve.wait_ge(ld_const, 16 * N_CONST_LD)
            v.tensor_copy(ident_bf[:, :], ident[:, :]).then_inc(const_bf, 1)
            v.tensor_scalar(neg_sinks[:, :], sinks[:, :], -1.0, None, ALU.mult).then_inc(const_neg, 1)

            def gained_lo(N, gain, c, k, idx):
                c0, n = CHUNKS[c]
                dve.wait_ge(N["hi"], idx + 1)
                v.scalar_tensor_tensor(out=h_lo[:, k, c0:c0 + n], in0=xT[:, k, c0:c0 + n], scalar=gains[:, gain, k:k + 1],
                                       in1=h_hi[:, k, c0:c0 + n].bitcast(F32), op0=ALU.mult, op1=ALU.subtract
                                       ).then_inc(N["lo"], 1)

            def mean(N, c, bank):
                c0, n = CHUNKS[c]
                dve.wait_ge(N["sum"], KT * (c + 1) if N is not N2 else KT * NCH)
                v.tensor_scalar(rstd[:, c0:c0 + n], ps[:, bank, 0:n], 1.0 / D_MODEL, EPS, ALU.mult, ALU.add
                                ).then_inc(N["mean"], 1)

            def invert(N, c):
                c0, n = CHUNKS[c]
                dve.wait_ge(N["sqrt"], c + 1)
                v.reciprocal(rstd[:, c0:c0 + n], rstd[:, c0:c0 + n]).then_inc(N["rstd"], 1)

            for c, (c0, n) in enumerate(CHUNKS):
                for t in range(c0 // P, (c0 + n) // P):
                    dve.wait_ge(x_turned, 2 * t + 2)
                    v.tensor_copy(xT[:, 4:8, t * P:(t + 1) * P],
                                  ps[:, 5 + 2 * (t % 2), :].rearrange("p (k n) -> p k n", k=4)).then_inc(x_kept_dve, 1)
                for k in range(KT):
                    gained_lo(N1, 0, c, k, KT * c + k)
                if c:
                    mean(N1, c - 1, SUMS[c - 1])
            mean(N1, NCH - 1, SUMS[NCH - 1])
            for c in range(NCH):
                invert(N1, c)

            def ffn_body(A, N, i, last=None):
                for s in range(6):
                    t, c = s // NCH, s % NCH
                    c0, n = CHUNKS[c]
                    b = s % 2
                    r = rstd[:, c0:c0 + n]
                    if t == 0:
                        dve.wait_ge(N["rstd"], c + 1)
                    dve.wait_ge(A["gu_done"], 6 * i + s + 1)
                    v.tensor_tensor(scaled_g[b][:, 0:n], r, ps[:, GU + 2 * b, 0:n], ALU.mult).then_inc(A["gate_rs"], 1)
                    v.tensor_tensor(scaled_u[b][:, 0:n], r, ps[:, GU + 2 * b + 1, 0:n], ALU.mult
                                    ).then_inc(A["up_rs"], 1)
                    dve.wait_ge(A["silu"], 6 * i + s + 1)
                    dve.wait_ge(A["up_rs"], GU_FREE + 6 * i + s + 1)
                    v.tensor_tensor(prod[b][:, 0:n], silu[b][:, 0:n], scaled_u[b][:, 0:n], ALU.mult
                                    ).then_inc(A["prod"], 1)
                    dve.wait_ge(A["hid_hi"], 6 * i + s + 1)
                    v.tensor_tensor(hid_lo[:, t, c0:c0 + n], prod[b][:, 0:n], hid_hi[:, t, c0:c0 + n].bitcast(F32),
                                    ALU.subtract).then_inc(A["hid_lo"], 1)
                for c, (c0, n) in enumerate(CHUNKS):
                    for k in range(KT):
                        m = KT * c + k
                        dve.wait_ge(A["dn_done"], DN_USED + 24 * i + m + 1)
                        v.scalar_tensor_tensor(out=xT[:, k, c0:c0 + n], in0=ps[:, DN + m % 4, 0:n], scalar=0.5,
                                               in1=xT[:, k, c0:c0 + n], op0=ALU.mult,
                                               op1=ALU.add).then_inc(A["dn_added"], 1)
                    if last:
                        last(c)

            def ffn(A, N, last):
                with dve.Fori(0, GROUPS - 1) as i:
                    ffn_body(A, N, i)
                ffn_body(A, N, GROUPS - 1, last)

            def to_mix(c):
                for k in range(KT):
                    gained_lo(NM, 1, c, k, KT * c + k)
                if c:
                    mean(NM, c - 1, SUMS[c - 1])
                if c == NCH - 1:
                    invert(NM, 0)
                    invert(NM, 1)

            ffn(A1, N1, to_mix)

            for c, (c0, n) in enumerate(CHUNKS):
                if c == 2:
                    mean(NM, c, SUMS[c])
                    invert(NM, c)
                dve.wait_ge(in_done, IN_USED + c + 1)
                dve.wait_ge(NM["rstd"], c + 1)
                v.tensor_tensor(rT[0:2 * RANK, c0:c0 + n], rstd[0:2 * RANK, c0:c0 + n], ps[0:2 * RANK, 4 + c, 0:n],
                                ALU.mult).then_inc(in_moved, 1)
            v.memset(rT[2 * RANK:2 * RANK + 1, :], 1.0).then_inc(G["ones"], 1)
            dve.wait_ge(NM["sum"], KT * NCH)
            v.memset(w_dec[:, :], 0.0).then_inc(G["zeroed"], 1)

            def in_unit(i, j, w):
                dve.wait_ge(in_stored[j], 16 + 16 * i)
                for c, (c0, n) in enumerate(CHUNKS):
                    dve.wait_ge(in_done, IN_USED + NCH * w + c + 1)
                    v.tensor_tensor(stage[j][:, c0:c0 + n], rstd[:, c0:c0 + n], ps[:, 4 + c, 0:n],
                                    ALU.mult).then_inc(in_moved, 1)

            fw, bw = slice(0, DK), slice(DK, P)

            def cumulate(h):
                dve.wait_ge(G["ln"], h + 1)
                v.scalar_tensor_tensor(out=gla_z[:, :], in0=gla_z[:, :], scalar=0.0, in1=gla_t[:, :],
                                       op0=ALU.min, op1=ALU.subtract).then_inc(G["log"], 1)
                dve.wait_ge(G["log"], h + 1)
                v.tensor_tensor_scan(gla_b[fw, :], reset[fw, :], gla_z[fw, :], 0.0, ALU.mult, ALU.add
                                     ).then_inc(G["scan"], 1)
                v.tensor_tensor_scan(gla_b[bw, ::-1], reset[bw, ::-1], gla_z[bw, ::-1], 0.0, ALU.mult, ALU.add
                                     ).then_inc(G["scan"], 1)
                dve.wait_ge(G["scan"], 2 * h + 2)
                for rows, edge in ((fw, C - 1), (bw, 0)):
                    bc = gla_b[rows, :].rearrange("p (n c) -> p n c", c=C)
                    v.tensor_tensor(gla_z[rows, :].rearrange("p (n c) -> p n c", c=C),
                                    bc[:, :, edge:edge + 1].to_broadcast([DK, TOK // C, C]), bc,
                                    ALU.subtract).then_inc(G["diff"], 1)

            dve.wait_ge(G["ld_tables"], 16)
            with dve.Fori(0, GLA_HEADS) as i:
                in_unit(i, 0, 3 * i + 1)
                in_unit(i, 1, 3 * i + 2)
                cumulate(i)
                in_unit(i, 2, 3 * i + 3)
            with dve.Fori(GLA_HEADS, IN_TILES // 3) as i:
                for j in range(3):
                    in_unit(i, j, 3 * i + (j + 1))

            for j in range(3):
                dve.wait_ge(in_stored[j], 16 + 16 * IN_TILES // 3)
            dve.wait_ge(in_done, IN_USED + NCH * (IN_TILES + 1))
            for a, b in zip(first_chunks, last_chunks):
                for t in gla_s:
                    v.memset(t[fw, :, a:a + 1], 0.0).then_inc(G["s_zeroed"], 1)
                    v.memset(t[bw, :, b:b + 1], 0.0).then_inc(G["s_zeroed"], 1)
            v.memset(gla_dec[:, :, :], 0.0).then_inc(G["s_zeroed"], 1)
            dve.wait_ge(G["ld_tables"], 32)

            def query(h):
                p = h % 2
                dve.wait_ge(e_ld[p], 48 * (h // 2 + 1))
                dve.wait_ge(q_ld[h % 3], 32 * (h // 3 + 1))
                v.scalar_tensor_tensor(out=gq[h % 3][:, :], in0=gq[h % 3][:, :], scalar=DK ** -0.5, in1=e_fw[p][:, :],
                                       op0=ALU.mult, op1=ALU.mult).then_inc(G["qe"], 1)

            def mask(h, chunks):
                a = gla_a[h % 2]
                for c in chunks:
                    c0, n = CHUNKS[c]
                    t0, t1 = c0 // P, (c0 + n) // P
                    dve.wait_ge(G["scores"], NCH * h + c + 1)
                    back = ps[:, 1, 0:n].rearrange("p (t i) -> p t i", i=P)
                    for d, out in ((0, a[:, t0:t1, :]), (1, back)):
                        v.tensor_tensor(out, ps[:, d, 0:n].rearrange("p (t i) -> p t i", i=P),
                                        masks[:, d:d + 1, :].to_broadcast([P, t1 - t0, P]), ALU.mult
                                        ).then_inc(G["masking"], 1)
                    dve.wait_ge(G["masking"], 2 * (NCH * h + c + 1))
                    v.tensor_tensor(a[:, t0:t1, :], a[:, t0:t1, :], back, ALU.add).then_inc(G["masked"], 1)

            query(0)
            query(1)
            mask(0, range(NCH))
            for h in range(GLA_HEADS):
                s = gla_s[h % 2]
                if h >= 2:
                    dve.wait_ge(G["o"], NCH * (h - 1))
                dve.wait_ge(G["u"], h + 1)
                for start in range(2):
                    for a, b in zip(first_chunks, last_chunks):
                        n0 = a + 1 + start
                        n = len(range(n0, b + 1, 2))
                        col = u_col(n0)
                        v.tensor_copy(s[bw, :, n0 - 1:b:2], psf[bw, col:col + n * DV].rearrange("p (n d) -> p d n", d=DV)
                                      ).then_inc(G["u_bw"], 1)
                if h + 1 < GLA_HEADS:
                    mask(h + 1, (0,))
                dve.wait_ge(G["decay"], 4 * h + 4)
                dve.wait_ge(G["u_bw"], 4 * h + 4)
                flat, dec = s[:, :, :].rearrange("p d n -> p (d n)"), gla_dec[:, :, :].rearrange("p d n -> p (d n)")
                v.tensor_tensor_scan(flat[bw, ::-1], dec[bw, ::-1], flat[bw, ::-1], 0.0, ALU.mult, ALU.add
                                     ).then_inc(G["state"], 1)
                dve.wait_ge(G["u_fw"], 4 * h + 4)
                v.tensor_tensor_scan(flat[fw, :], dec[fw, :], flat[fw, :], 0.0, ALU.mult, ALU.add
                                     ).then_inc(G["state"], 1)
                if h + 1 < GLA_HEADS:
                    mask(h + 1, (1, 2))
                if h + 2 < GLA_HEADS:
                    query(h + 2)
            dve.wait_ge(gn["sum"], GLA_HEADS)
            v.tensor_scalar(grs[:, :], psf[:, GLA_SUMS:GLA_SUMS + GLA_HEADS * TT], 1.0 / DV, EPS, ALU.mult, ALU.add
                            ).then_inc(gn["mean"], 1)
            dve.wait_ge(gn["sqrt"], 1)
            v.reciprocal(grs[:, :], grs[:, :]).then_inc(gn["rstd"], 1)

            dve.wait_ge(T["ld"], 7 * 16)
            v.memset(kT[:, :, 0:P], 0.0).then_inc(T["pads"], 1)
            v.memset(kT[:, :, P + TOK:], 0.0).then_inc(T["pads"], 1)
            v.memset(vN[:, 0, :], 0.0).then_inc(T["pads"], 1)
            v.memset(vN[:, TT + 1, :], 0.0).then_inc(T["pads"], 1)
            keys = kT[:, :, P:P + TOK]
            v.tensor_tensor(keys, keys, cos[:, :].unsqueeze(1).to_broadcast([HD, KV, TOK]), ALU.mult
                            ).then_inc(T["cosd"], 1)
            v.tensor_tensor(k_sw[:, :, :], k_sw[:, :, :], sin[:, :].unsqueeze(1).to_broadcast([HD, KV, TOK]), ALU.mult
                            ).then_inc(T["sind"], 1)
            dve.wait_ge(T["cosd"], 1)
            dve.wait_ge(T["sind"], 1)
            v.tensor_tensor(keys, keys, k_sw[:, :, :], ALU.add).then_inc(T["keys"], 1)

            for h in range(GLA_HEADS):
                for c, (c0, n) in enumerate(CHUNKS):
                    r = NCH * h + c
                    o = o_raw[:, 4 + h, c0:c0 + n]
                    dve.wait_ge(gn["spread"], r + 1)
                    dve.wait_ge(gn["gated"], h + 1)
                    v.scalar_tensor_tensor(out=o, in0=o, scalar=gla_gain[:, 0:1], in1=ps[:, 2 + r % 6, 0:n],
                                           op0=ALU.mult, op1=ALU.mult).then_inc(gn["scaled"], 1)

            def attend(u, r, first, drain):
                st = stats[r % 4]
                t = r % 4
                if not drain:
                    dve.wait_ge(T["s"], S_FREE + u + 1)
                    v.reduce_max(st[:, MX, :], ps[:, 2 * (r % 2):2 * (r % 2) + 2, 0:3 * P], AX.X).then_inc(T["max"], 1)
                    dve.wait_ge(T["max"], u + 1)
                    v.scalar_tensor_tensor(out=st[:, NEGM, :], in0=st[:, MX, :], scalar=-HD ** -0.5,
                                           in1=neg_sinks[:, 2 * t:2 * t + 2], op0=ALU.mult, op1=ALU.min
                                           ).then_inc(T["negm"], 1)
                    dve.wait_ge(T["negm"], u + 1)
                    v.tensor_tensor(st[:, DSINK, :], st[:, NEGM, :], sinks[:, 2 * t:2 * t + 2], ALU.add
                                    ).then_inc(T["dsink"], 1)
                if not (first and r < 3) and not (drain and r >= 3):
                    old = stats[(r - 3) % 4]
                    dve.wait_ge(T["pv"], u - 2)
                    if not (first and r < 5):
                        dve.wait_ge(T["oT"], u - 4)
                    for e in range(2):
                        v.tensor_scalar(o_nat[(r - 3) % 2][:, e * HD:(e + 1) * HD], ps[:, 6, e * HD:(e + 1) * HD],
                                        old[:, RDEN, e:e + 1], None, ALU.mult).then_inc(T["o_nat"], 1)
                if not (first and r < 2) and not (drain and r >= 2):
                    dve.wait_ge(T["turned"], u - 1)
                    v.tensor_copy(probsT[:, 1, :, :],
                                  ps[:, 5, 0:3 * P].rearrange("p (j q) -> p j q", j=3)).then_inc(T["pT_dve"], 1)
                if not (first and r < 1) and not (drain and r >= 1):
                    new = stats[(r - 1) % 4]
                    dve.wait_ge(T["es"], u)
                    v.tensor_tensor(new[:, RDEN, :], new[:, SUM, :], new[:, ESINK, :], ALU.add).then_inc(T["den"], 1)
                    dve.wait_ge(T["den"], u)
                    v.reciprocal(new[:, RDEN, :], new[:, RDEN, :]).then_inc(T["rden"], 1)

            dve.wait_ge(const_neg, 1)
            for r in range(8):
                attend(r, r, True, False)
            with dve.Fori(1, TT // 2) as i:
                for r in range(8):
                    attend(8 * i + r, r, False, False)
            for r in range(4):
                attend(TT // 2 * 8 + r, r, False, True)

            for c, (c0, n) in enumerate(CHUNKS):
                for k in range(KT):
                    dve.wait_ge(o_hi, KT * c + k + 1)
                    v.tensor_tensor(h_lo[:, k, c0:c0 + n], o_raw[:, k, c0:c0 + n], h_hi[:, k, c0:c0 + n].bitcast(F32),
                                    ALU.subtract).then_inc(o_lo, 1)

            for n in range(KT):
                for c, (c0, w) in enumerate(CHUNKS):
                    dve.wait_ge(out_done, NCH * n + c + 1)
                    v.tensor_tensor(xT[:, n, c0:c0 + w], ps[:, c, 0:w], xT[:, n, c0:c0 + w], ALU.add
                                    ).then_inc(out_added, 1)
                    if n == KT - 1 and c == 0:
                        for k in range(KT):
                            gained_lo(N2, 2, 0, k, k)
            for c in range(1, NCH):
                for k in range(KT):
                    gained_lo(N2, 2, c, k, KT * c + k)
            for c in range(NCH):
                mean(N2, c, 4 + c)
            for c in range(NCH):
                invert(N2, c)
            def normalize(c):
                c0, n = CHUNKS[c]
                dve.wait_ge(NF["rstd"], c + 1)
                for k in range(KT):
                    v.scalar_tensor_tensor(out=normed[:, k, c0:c0 + n], in0=xT[:, k, c0:c0 + n],
                                           scalar=gains[:, 3, k:k + 1], in1=rstd[:, c0:c0 + n],
                                           op0=ALU.mult, op1=ALU.mult).then_inc(y_scaled, 1)

            def to_final(c):
                if c == 1:
                    mean(NF, 0, SUMS[0])
                    invert(NF, 0)

            ffn(A2, N2, to_final)
            normalize(0)
            mean(NF, 1, SUMS[1])
            mean(NF, 2, SUMS[2])
            invert(NF, 1)
            invert(NF, 2)
            normalize(1)
            normalize(2)

        @block.tensor
        def _(pe):
            mm = nc.tensor.matmul
            for A in (A1, A2):
                pe.sem_inc(A["dn_done"], DN_USED)
            pe.sem_inc(in_done, IN_USED)
            pe.sem_inc(G["gate"], NCH)
            pe.sem_inc(T["s"], S_FREE)

            def mm3(out, wslot, wk, rhs_hi, rhs_lo, first, last, width=P):
                hi, lo = w_hi[wslot][:, wk, 0:width], w_lo[wslot][:, wk, 0:width]
                mm(out, hi, rhs_hi, start=first, stop=False)
                mm(out, hi, rhs_lo, start=False, stop=False)
                return mm(out, lo, rhs_hi, start=False, stop=last)

            def project(bank, c, wslot, width=P):
                c0, n = CHUNKS[c]
                for k in range(KT):
                    last = mm3(ps[0:width, bank, 0:n], wslot, k, h_hi[:, k, c0:c0 + n], h_lo[:, k, c0:c0 + n],
                               k == 0, k == KT - 1, width)
                return last

            def sums(N, c, bank):
                if c == 2:
                    pe.wait_ge(N["mean"], 1)
                for k in range(KT):
                    pe.wait_ge(N["square"], KT * c + k + 1)
                    mm(ps[:, bank, 0:CHUNKS[c][1]], ones[:, :], square[(KT * c + k) % 2][:, 0:CHUNKS[c][1]],
                       start=(k == 0), stop=(k == KT - 1)).then_inc(N["sum"], 1)

            def h_ready(N, c):
                pe.wait_ge(N["lo"], KT * (c + 1))

            def ffn_body(A, N, base, i, last=None):
                for s in range(6):
                    t, c = s // NCH, s % NCH
                    g_slot, u_slot = 2 * t % SPLIT, (2 * t + 1) % SPLIT
                    if t == 0:
                        h_ready(N, c)
                    if s == 1:
                        pe.wait_ge(N["mean"], NCH)
                    if c == 0:
                        pe.wait_ge(w_lo_ready, LO + base + 6 * i + 2 * t + 1)
                    pe.wait_ge(A["up_rs"], 6 * i + s + 1)
                    done = project(GU + 2 * (s % 2), c, g_slot)
                    if c == NCH - 1:
                        done.then_inc(A["gate_used"], 1)
                    if c == 0:
                        pe.wait_ge(w_lo_ready, LO + base + 6 * i + 2 * t + 2)
                    project(GU + 2 * (s % 2) + 1, c, u_slot).then_inc(A["gu_done"], 1)
                pe.wait_ge(w_lo_ready, LO + base + 6 * i + 6)
                for c, (c0, n) in enumerate(CHUNKS):
                    pe.wait_ge(A["hid_lo"], 6 * i + NCH + c + 1)
                    for k in range(KT):
                        m = KT * c + k
                        pe.wait_ge(A["dn_added"], 24 * i + m + 1)
                        for t in range(2):
                            done = mm3(ps[:, DN + m % 4, 0:n], (4 + t) % SPLIT, k, hid_hi[:, t, c0:c0 + n],
                                       hid_lo[:, t, c0:c0 + n], t == 0, t == 1)
                        done.then_inc(A["dn_done"], 1)
                    if last and c:
                        sums(last, c - 1, SUMS[c - 1])

            def ffn(A, N, base, after):
                with pe.Fori(0, GROUPS - 1) as i:
                    ffn_body(A, N, base, i)
                ffn_body(A, N, base, GROUPS - 1, after)

            pe.wait_ge(ld_const, 16 * N_CONST_LD)
            pe.wait_ge(const_ones, 1)
            for c, (c0, n) in enumerate(CHUNKS):
                for t in range(c0 // P, (c0 + n) // P):
                    if t * P == c0:
                        pe.wait_ge(x_loaded[c], 16 * n // P)
                    if t >= 2:
                        pe.wait_ge(x_kept_act, t - 1)
                        pe.wait_ge(x_kept_dve, t - 1)
                    for half in range(2):
                        for k in range(4):
                            last = nc.tensor.transpose(ps[:, 4 + 2 * (t % 2) + half, k * P:(k + 1) * P],
                                                       x_in[t][:, (4 * half + k) * P:(4 * half + k + 1) * P],
                                                       ident[:, :])
                        last.then_inc(x_turned, 1)
                if c:
                    sums(N1, c - 1, SUMS[c - 1])
            sums(N1, NCH - 1, SUMS[NCH - 1])
            ffn(A1, N1, 0, NM)

            def in_unit(slot, w, width=P):
                pe.wait_ge(w_lo_ready, LO + U_IN + w + 1)
                for c in range(NCH):
                    if c == 2 and width < P:
                        sums(NM, c, SUMS[c])
                    h_ready(NM, c)
                    pe.wait_ge(in_moved, NCH * w + c + 1)
                    project(4 + c, c, slot, width).then_inc(in_done, 1)

            def gates(h):
                pe.wait_ge(G["w_ld"], 64 * h + 64)
                pe.wait_ge(G["z"], NCH * h + GATE_FREE)
                for c, (c0, n) in enumerate(CHUNKS):
                    mm(ps[:, c, 0:n], w_dec[:, :], rT[:, c0:c0 + n], start=True, stop=True).then_inc(G["gate"], 1)

            in_unit(0, 0, 2 * RANK)
            pe.wait_ge(in_moved, IN_FREE + NCH)
            pe.wait_ge(G["ones"], 1)
            pe.wait_ge(NM["mean"], NCH)
            with pe.Fori(0, GLA_HEADS) as i:
                in_unit(1, 3 * i + 1)
                gates(i)
                in_unit(2, 3 * i + 2)
                in_unit(0, 3 * i + 3)
            with pe.Fori(GLA_HEADS, IN_TILES // 3) as i:
                for j in range(3):
                    in_unit((1 + j) % 3, 3 * i + (j + 1))

            pe.wait_ge(in_moved, IN_FREE + NCH * (IN_TILES + 1))

            def turn(h, name, done, before, x):
                for c, (c0, n) in enumerate(CHUNKS):
                    if before:
                        pe.wait_ge(G[before], NCH * h + c + 1)
                    for t in range(c0 // P, (c0 + n) // P):
                        last = nc.tensor.transpose(ps[:, 4 + c, t * P - c0:(t + 1) * P - c0],
                                                   x[:, t * P:(t + 1) * P], ident[:, :])
                    last.then_inc(G[name], 1)

            def scores(h, c):
                c0, n = CHUNKS[c]
                pe.wait_ge(G["qe"], h + 1)
                pe.wait_ge(G["ke"], h + 1)
                if NCH * h + c:
                    pe.wait_ge(G["masked"], NCH * h + c)
                for t in range(c0 // P, (c0 + n) // P):
                    for d in range(2):
                        rows = slice(d * DK, (d + 1) * DK)
                        last = mm(ps[:, d, t * P - c0:(t + 1) * P - c0], k_in[h % 2][rows, t * P:(t + 1) * P],
                                  gq[h % 3][rows, t * P:(t + 1) * P], start=True, stop=True)
                last.then_inc(G["scores"], 1)

            def prepare(h):
                scores(h, 0)
                pe.wait_ge(G["ld_v"], 16 * (h + 1))
                if h:
                    pe.wait_ge(G["u_fw"], 4 * h)
                    pe.wait_ge(G["u_bw"], 4 * h)
                turn(h, "vT", "vN", None, gvT)
                pe.wait_ge(G["ks"], h + 1)
                turn(h, "kT", "kN", "vN", k_out[h % 2])
                scores(h, 1)
                scores(h, 2)

            def head_sums(h):
                pe.wait_ge(gn["square"], h + 1)
                for t in range(TT):
                    last = mm(psf[:, GLA_SUMS + h * TT + t:GLA_SUMS + h * TT + t + 1], gsq[h][:, t * P:(t + 1) * P],
                              ones[:, 0:1], start=True, stop=True)
                last.then_inc(gn["sum"], 1)

            prepare(0)
            for h in range(GLA_HEADS):
                p = h % 2
                pe.wait_ge(G["kN"], NCH * (h + 1))
                if h:
                    pe.wait_ge(G["o_kept"], NCH * h)
                for parity in range(2):
                    for n in range(parity, TOK // C, 2):
                        rows = slice(parity * C, parity * C + C)
                        last = mm(psf[:, u_col(n):u_col(n) + DV], gla_kn[rows, n // 2, :], gla_vn[p][rows, n // 2, :],
                                  start=True, stop=True)
                last.then_inc(G["u"], 1)
                if h + 1 < GLA_HEADS:
                    prepare(h + 1)
                pe.wait_ge(G["u_bw"], 4 * (h + 1))
                pe.wait_ge(G["u_fw"], 4 * (h + 1))
                if h:
                    head_sums(h - 1)
                pe.wait_ge(G["masked"], NCH * (h + 1))
                pe.wait_ge(G["state"], 2 * (h + 1))
                for c, (c0, n) in enumerate(CHUNKS):
                    for t in range(c0 // P, (c0 + n) // P):
                        o = ps[:, O_BANKS[c], t * P - c0:(t + 1) * P - c0]
                        mm(o, gla_vn[p][:, t, :], gla_a[p][:, t, :], start=True, stop=False)
                        for e in range(2):
                            m = 2 * t + e
                            last = mm(o[:, e * C:(e + 1) * C], gla_s[p][:, :, m],
                                      gq[h % 3][:, m * C:(m + 1) * C], start=False, stop=(e == 1))
                    last.then_inc(G["o"], 1)
            head_sums(GLA_HEADS - 1)
            pe.wait_ge(T["ld"], 7 * 16)
            for c, (c0, n) in enumerate(CHUNKS):
                for t in range(c0 // P, (c0 + n) // P):
                    last = nc.tensor.transpose(ps[:, 4 + c, t * P - c0:(t + 1) * P - c0],
                                               vT[:, t * P:(t + 1) * P], ident[:, :])
                last.then_inc(T["vT"], 1)
            pe.wait_ge(T["vN"], 3)
            pe.wait_ge(gn["rstd"], 1)
            for h in range(GLA_HEADS):
                for c, (c0, n) in enumerate(CHUNKS):
                    r = NCH * h + c
                    if r >= 6:
                        pe.wait_ge(gn["scaled"], r - 5)
                    for t in range(c0 // P, (c0 + n) // P):
                        last = mm(ps[:, 2 + r % 6, t * P - c0:(t + 1) * P - c0],
                                  grs[:, h * TT + t:h * TT + t + 1].to_broadcast([P, P]), ident[:, :],
                                  start=True, stop=True)
                    last.then_inc(gn["spread"], 1)
            pe.wait_ge(gn["scaled"], NCH * GLA_HEADS)

            pe.wait_ge(const_bf, 1)
            pe.wait_ge(T["pads"], 4)
            pe.wait_ge(T["keys"], 1)
            pe.wait_ge(T["window"], 1)
            pe.wait_ge(T["vN"], 3)

            def attend(u, i, r, first, drain):
                if not drain:
                    t, blk = r % 4, 2 * i + r // 4
                    pe.wait_ge(T["qrot"], blk + 1)
                    pe.wait_ge(T["p"], 2 * u + 2)
                    for e in range(2):
                        bank = 2 * (r % 2) + e
                        edges = ps[:, bank, 0:4 * P].rearrange("p (a s q) -> p a s q", a=2, s=2)[:, :, 0, :]
                        mm(edges, ident_bf[:, :], window[:, bass.ds(blk, 1), :, :].rearrange("p b s k -> p (b s) k"),
                           start=True, stop=False, skip_group_check=True)
                        last = mm(ps[:, bank, 0:3 * P], q_rot[r // 4][:, 2 * t + e, :],
                                  kT[:, 2 * t // HPG, bass.ds(blk * P, 3 * P)], start=False, stop=True, skip_group_check=True)
                    last.then_inc(T["s"], 1)
                if not (first and r < 3) and not (drain and r >= 3):
                    blk = 2 * i + (r - 3) // 4
                    pe.wait_ge(T["pT_act"], PT_FREE + u - 2)
                    pe.wait_ge(T["pT_dve"], PT_FREE + u - 2)
                    pe.wait_ge(T["o_nat"], 2 * u - 4)
                    g = 2 * ((r - 3) % 4) // HPG
                    for e in range(2):
                        for j in range(3):
                            last = mm(ps[:, 6, e * HD:(e + 1) * HD], probsT[:, e, j, :],
                                      vN[:, bass.ds(blk + j, 1), g * HD:(g + 1) * HD].rearrange("p a d -> p (a d)"),
                                      start=(j == 0), stop=(j == 2))
                    last.then_inc(T["pv"], 1)
                if not (first and r < 2) and not (drain and r >= 2):
                    pe.wait_ge(T["p"], P_FREE + 2 * u - 2)
                    pe.wait_ge(T["pT_act"], u - 1)
                    pe.wait_ge(T["pT_dve"], u - 1)
                    for e in range(2):
                        for j in range(3):
                            last = nc.tensor.transpose(ps[:, 4 + e, j * P:(j + 1) * P],
                                                       probs[(r - 2) % 4][:, e, j * P:(j + 1) * P], ident[:, :])
                    last.then_inc(T["turned"], 1)
                if not (first and r < 4):
                    pe.wait_ge(T["o_nat"], ON_FREE + 2 * u - 6)
                    pe.wait_ge(T["o_kept"], u - 3)
                    nc.tensor.transpose(ps[:, 7, 0:P], o_nat[(r - 4) % 2][:, :], ident[:, :]).then_inc(T["oT"], 1)

            for r in range(8):
                attend(r, 0, r, True, False)
            with pe.Fori(1, TT // 2) as i:
                for r in range(8):
                    attend(8 * i + r, i, r, False, False)
            for r in range(4):
                attend(TT // 2 * 8 + r, TT // 2, r, False, True)

            def out_unit(n, slot):
                pe.wait_ge(w_lo_ready, LO + U_OUT + n + 1)
                for c in range(NCH):
                    pe.wait_ge(o_lo, KT * (c + 1))
                    pe.wait_ge(out_added, NCH * n + c + 1)
                    project(c, c, slot).then_inc(out_done, 1)
                    if c == 0 and n:
                        tile_sums(n - 1)

            def tile_sums(k):
                for c, (_, n) in enumerate(CHUNKS):
                    pe.wait_ge(N2["square"], NCH * k + c + 1)
                    mm(ps[:, 4 + c, 0:n], ones[:, :], square[c][:, 0:n], start=(k == 0), stop=(k == KT - 1)
                       ).then_inc(N2["sum"], 1)

            for n in range(KT):
                out_unit(n, (U_OUT + n) % SPLIT)
            tile_sums(KT - 1)
            ffn(A2, N2, U_FFN2, NF)
            sums(NF, 2, SUMS[2])
            for t in range(TT):
                pe.wait_ge(y_scaled, KT * (1 + t // 4))
                if t >= 2:
                    pe.wait_ge(y_kept, 2 * t - 2)
                for half in range(2):
                    for k in range(4):
                        last = nc.tensor.transpose(ps[:, 4 + 2 * (t % 2) + half, k * P:(k + 1) * P],
                                                   normed[:, 4 * half + k, t * P:(t + 1) * P], ident[:, :])
                    last.then_inc(y_turned, 1)


def shape_constants():
    half = HD // 2
    inv_freq = np.float32(10000.0) ** (-np.arange(half, dtype=np.float32) / np.float32(half))
    pos = np.concatenate([np.arange(s, dtype=np.float32) for s in SEQS])
    ang = inv_freq[:, None] * pos[None, :]
    cos = np.concatenate([np.cos(ang), np.cos(ang)]).astype(np.float32)
    sin = np.concatenate([-np.sin(ang), np.sin(ang)]).astype(np.float32)
    window = np.zeros((P, TT, 2, P), np.float32)
    q, k = np.arange(P)[:, None], np.arange(P)[None, :]
    first = [0, SEQS[0] // P]
    last = [SEQS[0] // P - 1, TT - 1]
    for b in range(TT):
        window[:, b, 0] = np.where((k >= q) & (b not in first), 0.0, NEG)
        window[:, b, 1] = np.where((k <= q) & (b not in last), 0.0, NEG)
    j, i = np.arange(P)[:, None], np.arange(P)[None, :]
    same = j // C == i // C
    masks = np.stack([same & (i >= j), same & (i < j)]).astype(np.float32)
    reset = np.ones((P, TOK), np.float32)
    reset[:DK, 0::C] = 0.0
    reset[DK:, C - 1::C] = 0.0
    return {"c_ident": np.eye(P, dtype=np.float32), "c_cos": cos, "c_sin": sin, "c_window": window,
            "c_gla_masks": masks, "c_reset": reset}


_INS = ["x_prompt", "x_sample", "norm_ffn1", "w_ffn1_gate", "w_ffn1_up", "w_ffn1_down", "norm_mix", "w_in",
        "attn_sink", "w_gla_decay_fwd", "b_gla_decay_fwd", "w_gla_decay_bwd", "b_gla_decay_bwd", "gla_out_norm",
        "w_out", "norm_ffn2", "w_ffn2_gate", "w_ffn2_up", "w_ffn2_down", "norm_final"]


def kernel(**inputs):
    import concourse.bacc as bacc
    from concourse.bass_utils import run_bass_kernel_spmd

    nc = bacc.Bacc("TRN2", target_bir_lowering=False, num_devices=1)
    arrays, args = {}, []
    for name, a in [(n, inputs[n]) for n in _INS] + list(shape_constants().items()):
        a = np.ascontiguousarray(a)
        arrays[f"in_{name}"] = a
        args.append(nc.dram_tensor(f"in_{name}", a.shape, mybir.dt.from_np(a.dtype), kind="ExternalInput").ap())
    for n, s in enumerate(SEQS):
        args.append(nc.dram_tensor(f"out_{n}", (1, s, D_MODEL), F32, kind="ExternalOutput").ap())
    args.append(nc.dram_tensor("proj", (ROW_E + 3 * GLA_HEADS * P, TOK), F32, kind="Internal").ap())
    build(nc, *args)
    r = run_bass_kernel_spmd(nc, [arrays], core_ids=[0])
    return tuple(r.results[0][f"out_{n}"] for n in range(2))
```
